# Optimizing a Trainium2 kernel written in Bass

```python
import jax, jax.numpy as jnp
from jax import lax
import numpy as np

D_MODEL = 1024
BATCH = 1
SEQ = 512
DEPTH = 1

N_MEM = 256
FOX_HEADS = 8
FOX_HEAD_DIM = D_MODEL // 16
FOX_WIDTH = FOX_HEADS * FOX_HEAD_DIM
Q_BLOCK = 128
HGRN_HEADS = 4
HGRN_KEY_DIM = D_MODEL // 16
HGRN_VAL_DIM = D_MODEL // 16
HGRN_KEY_WIDTH = HGRN_HEADS * HGRN_KEY_DIM
HGRN_WIDTH = HGRN_HEADS * HGRN_VAL_DIM
HGRN_CHUNK = 16
CONV_CH = D_MODEL // 4
CONV_GROUPS = 4
CONV_WIDTH = 31
MIX_WIDTH = FOX_WIDTH + HGRN_WIDTH + CONV_CH
IN_SIZES = (FOX_WIDTH, FOX_WIDTH, FOX_WIDTH, FOX_HEADS,
            HGRN_KEY_WIDTH, HGRN_KEY_WIDTH, HGRN_WIDTH, HGRN_WIDTH,
            CONV_CH, CONV_CH)
IN_WIDTH = 3 * FOX_WIDTH + FOX_HEADS + 2 * HGRN_KEY_WIDTH + 2 * HGRN_WIDTH + 2 * CONV_CH
XATT_HEADS = 4
XATT_HEAD_DIM = D_MODEL // XATT_HEADS
N_GROUPS = 4
EXPERTS_PER_GROUP = 4
EXPERT_TOPK = 2
EXPERT_FF = D_MODEL // 4
EPS = 1e-6

kernel_name = "hybrid_fox_hgrn2_conformer_hmoe"

def rmsnorm(x, g):
    xf = x.astype(jnp.float32)
    y = xf * lax.rsqrt(jnp.mean(xf * xf, axis=-1, keepdims=True) + EPS)
    return (y * g.astype(jnp.float32)).astype(x.dtype)

def split_columns(y, sizes):
    out, start = [], 0
    for n in sizes:
        out.append(y[..., start:start + n])
        start += n
    return out

def forgetting_attention(q, k, v, log_f):
    B, H, S, d = q.shape
    c = jnp.cumsum(log_f, axis=-1)
    nb = S // Q_BLOCK
    qb = q.reshape(B, H, nb, Q_BLOCK, d).transpose(2, 0, 1, 3, 4)
    cb = c.reshape(B, H, nb, Q_BLOCK).transpose(2, 0, 1, 3)
    qpos = jnp.arange(S, dtype=jnp.int32).reshape(nb, Q_BLOCK)
    kpos = jnp.arange(S, dtype=jnp.int32)
    scale = d ** -0.5

    def block(args):
        qi, ci, pi = args
        s = jnp.einsum('bhqd,bhkd->bhqk', qi, k).astype(jnp.float32) * scale
        s = s + (ci[..., None] - c[:, :, None, :])
        s = jnp.where(pi[:, None] >= kpos[None, :], s, -jnp.inf)
        p = jax.nn.softmax(s, axis=-1)
        return jnp.einsum('bhqk,bhkd->bhqd', p.astype(v.dtype), v)

    out = lax.map(block, (qb, cb, qpos))
    return out.transpose(1, 2, 0, 3, 4).reshape(B, H, S, d)

def hgrn2_recurrence(q, f_pre, v, lb):
    B, S, H, K = q.shape
    V = v.shape[-1]
    C = HGRN_CHUNK
    N = S // C
    f = lb + (1.0 - lb) * jax.nn.sigmoid(f_pre.astype(jnp.float32))
    g = jnp.log(f)
    k = 1.0 - f

    def chunks(t):
        return t.reshape(B, N, C, H, t.shape[-1]).transpose(0, 3, 1, 2, 4)

    qc = chunks(q.astype(jnp.float32))
    kc = chunks(k)
    vc = chunks(v.astype(jnp.float32))
    b = jnp.cumsum(chunks(g), axis=3)
    b_last = b[:, :, :, -1:, :]
    b_mid = b[:, :, :, C // 2:C // 2 + 1, :]
    attn = jnp.einsum('bhncK,bhnsK->bhncs', qc * jnp.exp(b - b_mid), kc * jnp.exp(b_mid - b))
    causal = jnp.tril(jnp.ones((C, C), dtype=bool))
    attn = jnp.where(causal, attn, 0.0)
    o_intra = jnp.einsum('bhncs,bhnsv->bhncv', attn, vc)
    u = jnp.einsum('bhncK,bhncv->bhnKv', kc * jnp.exp(b_last - b), vc)
    decay = jnp.exp(b_last[:, :, :, 0, :])

    def step(state, inp):
        dec, uu = inp
        return state * dec[..., None] + uu, state

    _, s_prev = lax.scan(step, jnp.zeros((B, H, K, V), jnp.float32),
                         (decay.transpose(2, 0, 1, 3), u.transpose(2, 0, 1, 3, 4)))
    s_prev = s_prev.transpose(1, 2, 0, 3, 4)
    o_inter = jnp.einsum('bhncK,bhnKv->bhncv', qc * jnp.exp(b), s_prev)
    o = (o_intra + o_inter).transpose(0, 2, 3, 1, 4).reshape(B, S, H, V)
    return o.astype(q.dtype)

def causal_depthwise_conv(a, w, bias):
    y = lax.conv_general_dilated(a, w[:, None, :].astype(a.dtype), window_strides=(1,),
                                 padding=[(CONV_WIDTH - 1, 0)],
                                 dimension_numbers=('NWC', 'WIO', 'NWC'),
                                 feature_group_count=a.shape[-1])
    return y + bias.astype(a.dtype)

def channel_group_norm(a, g, bias):
    B, S, C = a.shape
    af = a.astype(jnp.float32).reshape(B, S, CONV_GROUPS, C // CONV_GROUPS)
    mu = jnp.mean(af, axis=-1, keepdims=True)
    var = jnp.mean(jnp.square(af - mu), axis=-1, keepdims=True)
    y = ((af - mu) * lax.rsqrt(var + EPS)).reshape(B, S, C)
    return (y * g + bias).astype(a.dtype)

def hybrid_mixer(h, w_in, fox_f_bias, fox_norm_g, lb, hgrn_norm_g,
                 conv_w, conv_b, conv_norm_g, conv_norm_b, w_out):
    B, S, _ = h.shape
    y = h @ w_in
    fq, fk, fv, ff, hq, hf, hi, hg, cu, cg = split_columns(y, IN_SIZES)
    to_heads = lambda t: t.reshape(B, S, FOX_HEADS, FOX_HEAD_DIM).transpose(0, 2, 1, 3)
    log_f = jax.nn.log_sigmoid((ff + fox_f_bias).astype(jnp.float32)).transpose(0, 2, 1)
    fo = forgetting_attention(to_heads(fq), to_heads(fk), to_heads(fv), log_f).transpose(0, 2, 1, 3)
    fo = rmsnorm(fo, fox_norm_g.reshape(FOX_HEADS, FOX_HEAD_DIM)).reshape(B, S, FOX_WIDTH)
    ho = hgrn2_recurrence(hq.reshape(B, S, HGRN_HEADS, HGRN_KEY_DIM),
                          hf.reshape(B, S, HGRN_HEADS, HGRN_KEY_DIM),
                          hi.reshape(B, S, HGRN_HEADS, HGRN_VAL_DIM),
                          lb.reshape(HGRN_HEADS, HGRN_KEY_DIM))
    ho = rmsnorm(ho, hgrn_norm_g.reshape(HGRN_HEADS, HGRN_VAL_DIM)).reshape(B, S, HGRN_WIDTH) * jax.nn.silu(hg)
    a = cu * jax.nn.sigmoid(cg)
    a = causal_depthwise_conv(a, conv_w, conv_b)
    co = jax.nn.silu(channel_group_norm(a, conv_norm_g, conv_norm_b))
    return jnp.concatenate([fo, ho, co], axis=-1) @ w_out

def cross_attention(h, mem_n, w_xq, w_xkv, w_xo):
    B, S, D = h.shape
    M = mem_n.shape[1]
    q = (h @ w_xq).reshape(B, S, XATT_HEADS, XATT_HEAD_DIM)
    k, v = jnp.split(mem_n @ w_xkv, 2, axis=-1)
    k = k.reshape(B, M, XATT_HEADS, XATT_HEAD_DIM)
    v = v.reshape(B, M, XATT_HEADS, XATT_HEAD_DIM)
    s = jnp.einsum('bshd,bmhd->bhsm', q, k).astype(jnp.float32) * (XATT_HEAD_DIM ** -0.5)
    p = jax.nn.softmax(s, axis=-1)
    o = jnp.einsum('bhsm,bmhd->bshd', p.astype(v.dtype), v).reshape(B, S, D)
    return o @ w_xo

def hierarchical_moe(h, w_group, b_group, w_router, b_router, w_gate, w_up, w_down):
    B, S, D = h.shape
    t = h.reshape(-1, D)
    n = t.shape[0]
    g_logits = (t @ w_group).astype(jnp.float32) + b_group
    p_group = jax.nn.softmax(g_logits, axis=-1)
    g_idx = jnp.argmax(g_logits, axis=-1)
    p_gsel = jnp.take_along_axis(p_group, g_idx[:, None], axis=1)[:, 0]
    e_logits = ((t @ w_router).astype(jnp.float32) + b_router).reshape(n, N_GROUPS, EXPERTS_PER_GROUP)
    e_sel = jnp.take_along_axis(e_logits, g_idx[:, None, None], axis=1)[:, 0]
    p_exp = jax.nn.softmax(e_sel, axis=-1)
    top_v, top_i = lax.top_k(p_exp, EXPERT_TOPK)
    top_v = top_v / jnp.sum(top_v, axis=-1, keepdims=True)
    e_w = jnp.sum(jax.nn.one_hot(top_i, EXPERTS_PER_GROUP, dtype=jnp.float32) * top_v[..., None], axis=1)
    combine = (p_gsel[:, None, None] * jax.nn.one_hot(g_idx, N_GROUPS, dtype=jnp.float32)[:, :, None]
               * e_w[:, None, :]).astype(t.dtype)
    out = jnp.zeros_like(t)
    for grp in range(N_GROUPS):
        hid = jax.nn.silu(jnp.einsum('nd,edf->nef', t, w_gate[grp])) * jnp.einsum('nd,edf->nef', t, w_up[grp])
        out = out + jnp.einsum('nef,efd->nd', hid * combine[:, grp, :, None], w_down[grp])
    return out.reshape(B, S, D)

def setup_inputs(seed: int = 0) -> dict:
    key = jax.random.key(seed)
    ks = jax.random.split(key, 32)
    nrm = lambda k, shape, scale: jax.random.normal(k, shape, jnp.float32) * scale
    gain = lambda k, shape: 1.0 + 0.02 * jax.random.normal(k, shape, jnp.float32)
    G, E, F = N_GROUPS, EXPERTS_PER_GROUP, EXPERT_FF
    return {
        "x": nrm(ks[0], (BATCH, SEQ, D_MODEL), 1.0),
        "mem": nrm(ks[1], (BATCH, N_MEM, D_MODEL), 1.0),
        "mix_norm_g": gain(ks[2], (DEPTH, D_MODEL)),
        "w_in": nrm(ks[3], (DEPTH, D_MODEL, IN_WIDTH), D_MODEL ** -0.5),
        "fox_f_bias": 2.0 + 0.5 * jax.random.normal(ks[4], (DEPTH, FOX_HEADS), jnp.float32),
        "fox_norm_g": gain(ks[5], (DEPTH, FOX_WIDTH)),
        "hgrn_lb_logits": nrm(ks[6], (DEPTH, HGRN_KEY_WIDTH), 0.5),
        "hgrn_norm_g": gain(ks[7], (DEPTH, HGRN_WIDTH)),
        "conv_w": nrm(ks[8], (DEPTH, CONV_WIDTH, CONV_CH), CONV_WIDTH ** -0.5),
        "conv_b": nrm(ks[9], (DEPTH, CONV_CH), 0.02),
        "conv_norm_g": gain(ks[10], (DEPTH, CONV_CH)),
        "conv_norm_b": nrm(ks[11], (DEPTH, CONV_CH), 0.02),
        "w_out": nrm(ks[12], (DEPTH, MIX_WIDTH, D_MODEL), MIX_WIDTH ** -0.5),
        "xatt_norm_g": gain(ks[13], (DEPTH, D_MODEL)),
        "mem_norm_g": gain(ks[14], (D_MODEL,)),
        "w_xq": nrm(ks[15], (DEPTH, D_MODEL, D_MODEL), D_MODEL ** -0.5),
        "w_xkv": nrm(ks[16], (DEPTH, D_MODEL, 2 * D_MODEL), D_MODEL ** -0.5),
        "w_xo": nrm(ks[17], (DEPTH, D_MODEL, D_MODEL), D_MODEL ** -0.5),
        "ffn_norm_g": gain(ks[18], (DEPTH, D_MODEL)),
        "w_group": nrm(ks[19], (DEPTH, D_MODEL, G), D_MODEL ** -0.5),
        "b_group": nrm(ks[20], (DEPTH, G), 0.01),
        "w_router": nrm(ks[21], (DEPTH, D_MODEL, G * E), D_MODEL ** -0.5),
        "b_router": nrm(ks[22], (DEPTH, G * E), 0.01),
        "w_gate": nrm(ks[23], (DEPTH, G, E, D_MODEL, F), D_MODEL ** -0.5),
        "w_up": nrm(ks[24], (DEPTH, G, E, D_MODEL, F), D_MODEL ** -0.5),
        "w_down": nrm(ks[25], (DEPTH, G, E, F, D_MODEL), F ** -0.5),
        "final_norm_g": gain(ks[26], (D_MODEL,)),
    }

def reference(x, mem, mix_norm_g, w_in, fox_f_bias, fox_norm_g, hgrn_lb_logits, hgrn_norm_g,
              conv_w, conv_b, conv_norm_g, conv_norm_b, w_out, xatt_norm_g, mem_norm_g,
              w_xq, w_xkv, w_xo, ffn_norm_g, w_group, b_group, w_router, b_router,
              w_gate, w_up, w_down, final_norm_g):
    mem_n = rmsnorm(mem, mem_norm_g)
    lb_all = jnp.cumsum(jax.nn.softmax(hgrn_lb_logits.astype(jnp.float32), axis=0), axis=0)
    lb_all = lb_all - lb_all[0:1]
    for l in range(DEPTH):
        x = x + hybrid_mixer(rmsnorm(x, mix_norm_g[l]), w_in[l], fox_f_bias[l], fox_norm_g[l],
                             lb_all[l], hgrn_norm_g[l], conv_w[l], conv_b[l],
                             conv_norm_g[l], conv_norm_b[l], w_out[l])
        x = x + cross_attention(rmsnorm(x, xatt_norm_g[l]), mem_n, w_xq[l], w_xkv[l], w_xo[l])
        x = x + hierarchical_moe(rmsnorm(x, ffn_norm_g[l]), w_group[l], b_group[l], w_router[l],
                                 b_router[l], w_gate[l], w_up[l], w_down[l])
    return rmsnorm(x, final_norm_g)


_drawn_inputs = setup_inputs


def setup_inputs(seed=0):
    import zlib

    import numpy as np

    out = dict(_drawn_inputs(seed))
    spreads = {}
    factors = {'fox_norm_g': 2.809,
     'hgrn_norm_g': 4.531,
     'conv_b': 3.532,
     'conv_norm_g': 3.328,
     'conv_norm_b': 3.244,
     'xatt_norm_g': 4.454,
     'mem_norm_g': 6.133,
     'b_group': 45.424,
     'b_router': 37.12,
     'final_norm_g': 7.796,
     'ffn_norm_g': 8.0}
    for name, (base, spread) in spreads.items():
        noise = np.random.default_rng([zlib.crc32(name.encode()), seed]).standard_normal(out[name].shape)
        drawn = base * np.exp(spread * noise) if base else spread * noise
        out[name] = __import__('jax').numpy.asarray(drawn.astype(out[name].dtype))
    for name, factor in factors.items():
        out[name] = (out[name] * factor).astype(out[name].dtype)
    return out
```

```python
from contextlib import ExitStack

import concourse.bass as bass
from concourse import mybir

F32 = mybir.dt.float32
F16 = mybir.dt.float16
BF16 = mybir.dt.bfloat16
I32 = mybir.dt.int32
U32 = mybir.dt.uint32
ALU = mybir.AluOpType
ACT = mybir.ActivationFunctionType
AX_X = mybir.AxisListType.X

P = 128
EPS = 1e-6
LOWEST = -3.0e38

D = 1024
S = 512
M = 256
FH, FD = 8, 64
FW = FH * FD
HH, HD = 4, 64
HW = HH * HD
CHUNK = 16
CC = 256
CW = 31
XH = 4
NG, NE = 4, 4
EX = NG * NE
FF = 256

DC = D // P
ST = S // P
MT = M // P
HP = HH // 2
NCH = S // CHUNK
CPT = P // CHUNK

C_FQ, C_FK, C_FV, C_FF = 0, FW, 2 * FW, 3 * FW
C_HQ = C_FF + FH
C_HF, C_HI, C_HG = C_HQ + HW, C_HQ + 2 * HW, C_HQ + 3 * HW
C_CU = C_HQ + 4 * HW
C_CG = C_CU + CC

R_MIX, R_XATT, R_MEM, R_FFN = 0, DC, 2 * DC, 3 * DC
R_FOX = 4 * DC
R_HG = R_FOX + FW // P
R_LB = R_HG + HW // P
R_CB = R_LB + HW // P
R_CNG = R_CB + CC // P
R_CNB = R_CNG + CC // P
R_CW = R_CNB + CC // P
NR = R_CW + CW * (CC // P)

SLOTS = 4
SLOT_COLS = 512
STAGE = 3


def build(nc, x, mem, mix_norm_g, w_in, fox_f_bias, fox_norm_g, hgrn_lb_logits, hgrn_norm_g,
          conv_w, conv_b, conv_norm_g, conv_norm_b, w_out, xatt_norm_g, mem_norm_g,
          w_xq, w_xkv, w_xo, ffn_norm_g, w_group, b_group, w_router, b_router,
          w_gate, w_up, w_down, final_norm_g, out):
    with ExitStack() as ctx:
        def sb(name, shape, dt=F32):
            return ctx.enter_context(nc.sbuf_tensor(name, shape, dt))

        def sem(name):
            return ctx.enter_context(nc.semaphore(name))

        x_sb = sb("x_sb", [P, ST, D])
        n_sb = sb("n_sb", [P, ST, D])
        hT = sb("hT", [P, DC, S])
        W = sb("W", [P, SLOTS, DC, SLOT_COLS])
        Dn = sb("Dn", [P, SLOTS, 2, D])
        A = sb("A", [P, 12288])
        states = sb("states", [P, NCH + 1, HD])

        identf = sb("identf", [P, P])
        identb = sb("identb", [P, P], BF16)
        causal = sb("causal", [P, P], BF16)
        chunkmask = sb("chunkmask", [P, P], I32)
        chunkcol = sb("chunkcol", [P, CPT])
        half64 = sb("half64", [P, P])
        scanmask = sb("scanmask", [P, S])
        mhalf = sb("mhalf", [P, 32])
        prow = sb("prow", [P, P])
        pc = sb("pc", [P, NR])
        lbv = sb("lbv", [P, 4 * HP])
        wff = sb("wff", [P, DC, FH])
        fbias = sb("fbias", [FH, 1])
        ss = sb("ss", [P, 4])
        rstd = sb("rstd", [P, 4])
        epsb = sb("epsb", [P, 1])

        qT = A[:, 0:2048].rearrange("p (c t) -> p c t", c=4)
        kT = A[:, 2048:4096].rearrange("p (c t) -> p c t", c=4)
        v = A[:, 4096:6144].rearrange("p (t n) -> p t n", t=ST)
        hqT = A[:, 6144:7168].rearrange("p (c t) -> p c t", c=HP)
        hfT = A[:, 7168:8192].rearrange("p (c t) -> p c t", c=HP)
        hgT = A[:, 8192:9216].rearrange("p (c t) -> p c t", c=HP)
        hv = A[:, 9216:10240].rearrange("p (t n) -> p t n", t=ST)
        cuT = A[:, 10240:11264].rearrange("p (c t) -> p c t", c=2)
        cgT = A[:, 11264:12288].rearrange("p (c t) -> p c t", c=2)
        fo = A[:, 6144:8192].rearrange("p (t n) -> p t n", t=ST)
        catT = n_sb[:, :, :].rearrange("p a b -> p (a b)").rearrange("p (c t) -> p c t", c=DC)
        scr = Dn[:, :, :, :].rearrange("p a b c -> p (a b c)").rearrange("p (n c t) -> p n c t", n=8, c=HP)
        hk, hgl, hb, hd1, he1, he2, he3, he4 = (scr[:, n] for n in range(8))
        khtok = hd1.rearrange("p c (t k) -> p c t k", t=ST)
        attm = Dn[:, 0:2].rearrange("p a b c -> p (a b c)")[:, 1024:3072].rearrange("p (h t s) -> p h t s", h=HH, t=ST)
        vexp = [hk.rearrange("p a (b n) -> p (a b n)", n=HD).rearrange("p (h n v) -> p h n v", h=2, n=CPT),
                hfT.rearrange("p a (b n) -> p (a b n)", n=HD).rearrange("p (h n v) -> p h n v", h=2, n=CPT)]
        hTf = hT[:, :, :].rearrange("p c t -> p (c t)")
        fs = [hTf[:, 0:512], hTf[:, 512:1024]]
        fpT = [hTf[:, 1024:1536], hTf[:, 1536:2048]]
        fnegc = [hTf[:, 2048:2560], hTf[:, 2560:3072]]
        fsq = hTf[:, 3072:3328].rearrange("p (t v) -> p t v", t=ST)
        lfa, lfb, ones8 = (catT[0:FH, c] for c in range(3))
        fmx = sb("fmx", [P, 32])
        fnm = sb("fnm", [P, 32])
        frs = sb("frs", [P, 32])
        frr = sb("frr", [P, 32])
        fss = sb("fss", [P, 32])
        frstd = sb("frstd", [P, 32])
        xqT = A[:, 0:4096].rearrange("p (c t) -> p c t", c=DC)
        xkT = A[:, 4096:6144].rearrange("p (c m) -> p c m", c=DC)
        xv = A[:, 6144:8192].rearrange("p (t n) -> p t n", t=MT)
        memT = A[:, 8192:10240].rearrange("p (c m) -> p c m", c=DC)
        mem_sb = A[:, 10240:12288].rearrange("p (t n) -> p t n", t=MT)
        xoT = catT
        xp = states[:, 0:16, :].rearrange("p a b -> p (a b)").rearrange("p (n m) -> p n m", n=4)
        xpT = Dn[:, 0].rearrange("p a b -> p (a b)").rearrange("p (c t) -> p c t", c=4)

        xg = A[:, 0:2048].rearrange("p (b d) -> p b d", b=2)
        xgT = A[:, 2048:4096].rearrange("p (b c t) -> p b c t", b=2, c=DC)
        sg = A[:, 4096:4608].rearrange("p (b f) -> p b f", b=2)
        hid = A[:, 4608:5120].rearrange("p (b f) -> p b f", b=2)
        hidT = A[:, 5120:5632].rearrange("p (b k t) -> p b k t", b=2, k=2)
        ysb = A[:, 5632:7680].rearrange("p (b d) -> p b d", b=2)
        fgain = A[:, 7680:8704]
        room = [8704]

        def small(*shape, dt=F32, parts=P):
            n = 1
            for k in shape:
                n *= k
            at = room[0]
            room[0] += n
            ap = A[0:parts, at:at + n]
            if dt is not F32:
                ap = ap.bitcast(dt)
            names = " ".join("abc"[:len(shape)])
            return ap.rearrange(f"p ({names}) -> p {names}", **{k: m for k, m in zip("abc", shape)}) if len(shape) > 1 else ap

        logits = small(ST, NG + EX)
        beats, ties = small(ST, 4, 4), small(ST, 4, 4)
        grank, ghot, erank, ehot = small(ST, 4), small(ST, 4), small(ST, 4), small(ST, 4)
        gtop, gsum, etop, esum = small(ST), small(ST), small(ST), small(ST)
        gexp, esel, eexp = small(ST, 4), small(ST, 4), small(ST, 4)
        spread = small(ST, 4, 4)
        picked, weight = small(ST, EX), small(ST, EX)
        pos, posm, slot, part = small(ST, EX), small(ST, EX), small(ST, EX), small(ST, EX)
        stop_, ssum_, w1st, w2nd = small(ST), small(ST), small(ST), small(ST)
        token_of = small(EX, dt=U32)
        slot1, slot2 = small(ST, dt=U32), small(ST, dt=U32)
        most = small(1)
        over = small(1, dt=I32)
        ov_token = small(1, dt=U32)
        pickedb = A[:, room[0]:room[0] + 32].bitcast(BF16).rearrange("p (t e) -> p t e", t=ST)
        srow = states[:, 17:, :].rearrange("p a b -> p (a b)")
        wgr = srow[:, 0:160].rearrange("p (c n) -> p c n", c=DC)
        rbias = srow[:, 160:180]
        ranks = srow[:, 192:320]
        before = srow[:, 320:384].bitcast(BF16)
        onesb = srow[:, 384:448].bitcast(BF16)
        lower = srow[:, 448:464].rearrange("p (i j) -> p i j", i=4)
        ebase = srow[:, 464:480]
        tokid = srow[:, 480:482].bitcast(F16)
        pick = hTf.bitcast(F16).rearrange("p (t e r) -> p t e r", t=ST, e=EX)
        ov_pick = hTf.bitcast(F16)[:, 0:ST * P].rearrange("p (t r) -> p t r", t=ST)
        ygath = hTf.rearrange("p (b k d) -> p b k d", b=2, k=2)

        n_dram = nc.dram_tensor("n_dram", (S, D), F32, kind="Internal").ap()
        y_dram = nc.dram_tensor("y_dram", (ST * EX * P, D), F32, kind="Internal").ap()
        y_rows = y_dram.rearrange("(e p) d -> e p d", p=P)

        PS = [ctx.enter_context(nc.psum_tensor(f"bank{i}", [P, 512], F32)) for i in range(8)]

        x_in = sem("x_in")
        params_in = sem("params_in")
        mem_in = sem("mem_in")
        w_in_slot = [sem(f"w_loaded{i}") for i in range(SLOTS)]
        const_step = sem("const_step")
        consts = sem("consts")
        pcol = sem("pcol")
        pcol_ps = sem("pcol_ps")
        lb_step = sem("lb_step")
        sq_done = sem("sq_done")
        ms_done = sem("ms_done")
        rstd_done = sem("rstd_done")
        n_done = sem("n_done")
        turned = sem("turned")
        turn_act = sem("turn_act")
        turn_dve = sem("turn_dve")
        proj = sem("proj")
        proj_out = sem("proj_out")
        conv_a = sem("conv_a")
        conv_y = sem("conv_y")
        cmean = sem("cmean")
        cdev = sem("cdev")
        cvar = sem("cvar")
        crs = sem("crs")
        cz = sem("cz")
        co_done = sem("co_done")
        hf_done = sem("hf_done")
        hg_log = sem("hg_log")
        hb_done = sem("hb_done")
        hd_done = sem("hd_done")
        he_done = sem("he_done")
        hprod = sem("hprod")
        kh_turned = sem("kh_turned")
        kh_out = sem("kh_out")
        vexp_done = sem("vexp_done")
        u_done = sem("u_done")
        state_step = sem("state_step")
        att_ps = sem("att_ps")
        att_zero = sem("att_zero")
        att_done = sem("att_done")
        ho_ps = sem("ho_ps")
        ho_sb = sem("ho_sb")
        ho_sq = sem("ho_sq")
        ho_ms = sem("ho_ms")
        ho_rs = sem("ho_rs")
        ho_step = sem("ho_step")
        lf_act = sem("lf_act")
        lf_dve = sem("lf_dve")
        negc_ps = sem("negc_ps")
        negc_sb = sem("negc_sb")
        qk_done = sem("qk_done")
        s_done = sem("s_done")
        m_done = sem("m_done")
        p_done = sem("p_done")
        pt_ps = sem("pt_ps")
        pt_act = sem("pt_act")
        pt_dve = sem("pt_dve")
        o_ps = sem("o_ps")
        o_sb = sem("o_sb")
        f_step = sem("f_step")
        f_ms = sem("f_ms")
        f_rstd = sem("f_rstd")
        fo_turned = sem("fo_turned")
        cat_out = sem("cat_out")
        wout_ps = sem("wout_ps")
        x1_done = sem("x1_done")
        xs_ps = sem("xs_ps")
        xm_done = sem("xm_done")
        xe_done = sem("xe_done")
        xr_done = sem("xr_done")
        xn_done = sem("xn_done")
        xpt_ps = sem("xpt_ps")
        xpt_sb = sem("xpt_sb")
        xo_ps = sem("xo_ps")
        xo_sb = sem("xo_sb")
        out_done = sem("out_done")
        f_normed = sem("f_normed")
        router_in = sem("router_in")
        router_const = sem("router_const")
        router_step = sem("router_step")
        logits_ps = sem("logits_ps")
        route = sem("route")
        soft_in = sem("soft_in")
        soft_out = sem("soft_out")
        picked_done = sem("picked_done")
        pos_ps = sem("pos_ps")
        pick_done = sem("pick_done")
        token_ps = sem("token_ps")
        token_done = sem("token_done")
        over_done = sem("over_done")
        slots_done = sem("slots_done")
        n_stored = sem("n_stored")
        dn_loaded = [sem(f"dn_loaded{i}") for i in range(SLOTS)]
        xg_in = [sem(f"xg_in{i}") for i in range(2)]
        xt_ps = sem("xt_ps")
        xt_sb = sem("xt_sb")
        gu_ps = sem("gu_ps")
        silu_done = sem("silu_done")
        hid_done = sem("hid_done")
        ht_ps = sem("ht_ps")
        ht_sb = sem("ht_sb")
        y_ps = sem("y_ps")
        y_act = sem("y_act")
        y_dve = sem("y_dve")
        y_stored = [sem(f"y_stored{i}") for i in range(2)]
        ov_pos = sem("ov_pos")
        ov_picked = sem("ov_picked")
        ov_token_ps = sem("ov_token_ps")
        ov_token_sb = sem("ov_token_sb")
        ov_xg = sem("ov_xg")
        ov_w = sem("ov_w")
        ov_xt_ps = sem("ov_xt_ps")
        ov_xt_sb = sem("ov_xt_sb")
        ov_gu = sem("ov_gu")
        ov_silu = sem("ov_silu")
        ov_hid = sem("ov_hid")
        ov_ht_ps = sem("ov_ht_ps")
        ov_ht_sb = sem("ov_ht_sb")
        ov_y_ps = sem("ov_y_ps")
        ov_y_sb = sem("ov_y_sb")
        ov_stored = sem("ov_stored")
        fin_in = [sem(f"fin_in{i}") for i in range(2)]
        fin_sum = sem("fin_sum")
        fin_sq = sem("fin_sq")
        fin_ms = sem("fin_ms")
        fin_root = sem("fin_root")
        fin_out = sem("fin_out")
        half_done = sem("half_done")
        ones_done = sem("ones_done")
        xs_step = sem("xs_step")
        fsteps = sem("fsteps")
        ctx_root = sem("root_step")
        croot = fpT
        hob = [he4[:, 0], he4[:, 1]]
        hrb = [he2[:, 0], he2[:, 1]]

        def rows(w):
            return w.rearrange("(c p) n -> p c n", p=P)

        win, wout, wxq, wxkv, wxo = rows(w_in[0]), rows(w_out[0]), rows(w_xq[0]), rows(w_xkv[0]), rows(w_xo[0])
        LOADS = [(win, C_CU), (win, C_HQ), (win, C_HI), (win, C_FQ), (win, C_FK), (win, C_FV),
                 (wout, 0), (wout, 512), (wxkv, 0), (wxkv, 512), (wxkv, 1024), (wxkv, 1536),
                 (wxq, 0), (wxq, 512), (wxo, 0), (wxo, 512)]

        def loaded(eng, n):
            eng.wait_ge(w_in_slot[n % SLOTS], 16 * (n // SLOTS + 1))

        GROUPS = {0: 4, 1: 9, 2: 15, 3: 19, 4: 23, 5: 27, 8: 31, 9: 35, 10: 37, 11: 39, 12: 43, 13: 47}

        def freed(n):
            return (proj, GROUPS[n]) if n in GROUPS else (wout_ps, 8 if n < 8 else 16)

        wg_e = w_gate.rearrange("l g e (c p) f -> (l g e) p c f", p=P)
        wu_e = w_up.rearrange("l g e (c p) f -> (l g e) p c f", p=P)
        wd_e = w_down.rearrange("l g e (k p) d -> (l g e) p k d", p=P)

        def load_gate_up(sp, e, s, done):
            sp.dma_start(W[:, s, :, 0:FF], wg_e[e]).then_inc(done, 16)
            sp.dma_start(W[:, s, :, FF:2 * FF], wu_e[e]).then_inc(done, 16)

        def gate_up_loaded(eng, s, turn_):
            eng.wait_ge(w_in_slot[s], 16 * len(LOADS) // SLOTS + 32 + 32 * turn_)

        block = ctx.enter_context(nc.Block())

        def experts_loads(sp):
            sp.wait_ge(x1_done, 8)
            for e in range(1, SLOTS):
                sp.dma_start(Dn[:, e], wd_e[e]).then_inc(dn_loaded[e], 16)
            for e in range(2):
                sp.wait_ge(*freed(12 + e))
                load_gate_up(sp, e, e, w_in_slot[e])
            sp.wait_ge(xo_ps, 2 * XH)
            sp.dma_start(Dn[:, 0], wd_e[0]).then_inc(dn_loaded[0], 16)
            for e in range(2, SLOTS):
                sp.wait_ge(*freed(12 + e))
                load_gate_up(sp, e, e, w_in_slot[e])
            sp.dma_start(fgain, final_norm_g.rearrange("(o d) -> o d", o=1).to_broadcast([P, D])).then_inc(router_in, 16)
            sp.wait_ge(n_done, 3 * ST + MT)
            sp.dma_start(n_dram.rearrange("(t p) d -> p t d", p=P), n_sb[:, :, :]).then_inc(n_stored, 16)

            def step(e, s, nxt):
                if nxt:
                    sp.wait_ge(gu_ps, e + 1)
                    load_gate_up(sp, e + SLOTS, s, w_in_slot[s])
                    sp.wait_ge(y_ps, 2 * e + 2)
                    sp.dma_start(Dn[:, s], wd_e[e + SLOTS]).then_inc(dn_loaded[s], 16)
                sp.wait_ge(y_act, e + 1)
                sp.wait_ge(y_dve, e + 1)
                sp.dma_start(y_rows[e], ysb[:, s % 2]).then_inc(y_stored[s % 2], 16)

            with sp.Fori(0, EX // SLOTS - 1) as i:
                for j in range(SLOTS):
                    step(i * SLOTS + j, j, True)
            for j in range(SLOTS):
                step(EX - SLOTS + j, j, False)

            sp.wait_ge(over_done, 1)
            with sp.If(sp.value_load(over[0:1, 0:1]) > 0):
                sp.wait_ge(y_ps, 2 * EX)
                with sp.Fori(0, (ST - 1) * EX) as k:
                    e = k % EX
                    sp.dma_start(W[:, 0, :, 0:FF], wg_e[e]).then_inc(ov_w, 16)
                    sp.dma_start(W[:, 0, :, FF:2 * FF], wu_e[e]).then_inc(ov_w, 16)
                    sp.dma_start(Dn[:, 0], wd_e[e]).then_inc(ov_w, 16)
                    sp.wait_ge(ov_y_sb, 2 * k + 2)
                    sp.dma_start(y_rows[k + EX], ysb[:, 0]).then_inc(ov_stored, 16)
            with sp.Else():
                pass
            for t in range(ST):
                sp.wait_ge(fin_out, t + 1)
                sp.dma_start(out[0, t * P:(t + 1) * P, :], n_sb[:, t, :]).then_inc(out_done, 16)
            sp.wait_ge(out_done, 16 * ST)

        @block.sync
        def _(sp):
            sp.dma_start(x_sb[:, :, :], x[0].rearrange("(t p) d -> p t d", p=P)).then_inc(x_in, 16)
            for n, (src, c0) in enumerate(LOADS):
                if n >= SLOTS:
                    sp.wait_ge(*freed(n - SLOTS))
                sp.dma_start(W[:, n % SLOTS], src[:, :, c0:c0 + SLOT_COLS]).then_inc(w_in_slot[n % SLOTS], 16)
                if n == 7:
                    sp.wait_ge(co_done, 2)
                    sp.dma_start(mem_sb, mem[0].rearrange("(t p) d -> p t d", p=P)).then_inc(mem_in, 16)
                    sp.wait_ge(ho_ps, 2)
                    sp.dma_start(wgr[:, :, 0:NG], rows(w_group[0])).then_inc(router_in, 16)
                    sp.dma_start(wgr[:, :, NG:], rows(w_router[0])).then_inc(router_in, 16)
                    sp.dma_start(rbias[:, 0:NG], b_group.to_broadcast([P, NG])).then_inc(router_in, 16)
                    sp.dma_start(rbias[:, NG:], b_router.to_broadcast([P, EX])).then_inc(router_in, 16)
            if STAGE == 3:
                experts_loads(sp)
            if STAGE < 3:
                sp.wait_ge(x1_done, 8 * STAGE)
                sp.dma_start(out[0].rearrange("(t p) d -> p t d", p=P), x_sb[:, :, :]).then_inc(out_done, 16)
                sp.wait_ge(out_done, 16)

        def experts_gathers(pool):
            root(pool, 3, ST)
            pool.wait_ge(n_stored, 16)
            pool.wait_ge(token_done, 1)
            for e in range(EX):
                if e >= 2:
                    pool.wait_ge(xt_ps, 2 * (e - 1))
                nc.gpsimd.indirect_dma_start(out=xg[:, e % 2, :], out_offset=None, in_=n_dram,
                                             in_offset=bass.IndirectOffsetOnAxis(ap=token_of[:, e:e + 1], axis=0)).then_inc(xg_in[e % 2], 16)
            def final_root(t):
                pool.wait_ge(fin_ms, t + 1)
                nc.gpsimd.tensor_tensor(rstd[:, t:t + 1], ss[:, t:t + 1], mhalf[:, 0:1], ALU.pow).then_inc(fin_root, 1)

            def combine_rows(written):
                pool.wait_ge(y_stored[0], 16 * EX // 2)
                pool.wait_ge(y_stored[1], 16 * EX // 2)
                pool.wait_ge(slots_done, 2)
                for t in range(ST):
                    if t >= 2:
                        pool.wait_ge(fin_sum, 2 * (t - 1))
                    for k, sl in enumerate((slot1, slot2)):
                        nc.gpsimd.indirect_dma_start(out=ygath[:, t % 2, k, :], out_offset=None, in_=written,
                                                     in_offset=bass.IndirectOffsetOnAxis(ap=sl[:, t:t + 1], axis=0)).then_inc(fin_in[t % 2], 16)
                    if t >= 2:
                        final_root(t - 2)
                final_root(ST - 2)
                final_root(ST - 1)

            pool.wait_ge(over_done, 1)
            with pool.If(pool.value_load(over[0:1, 0:1]) > 0):
                pool.wait_ge(xt_ps, 2 * EX)
                for k in range((ST - 1) * EX):
                    pool.wait_ge(ov_token_sb, k + 1)
                    nc.gpsimd.indirect_dma_start(out=xg[:, 0, :], out_offset=None, in_=n_dram,
                                                 in_offset=bass.IndirectOffsetOnAxis(ap=ov_token[:, 0:1], axis=0)).then_inc(ov_xg, 16)
                pool.wait_ge(ov_stored, 16 * (ST - 1) * EX)
                combine_rows(y_dram)
            with pool.Else():
                combine_rows(y_dram[0:EX * P, :])

        def root(pool, stage, k):
            pool.wait_ge(ms_done, stage + 1)
            nc.gpsimd.tensor_tensor(rstd[:, 0:k], ss[:, 0:k], mhalf[:, 0:k], ALU.pow).then_inc(rstd_done, 1)

        @block.gpsimd
        def _(pool):
            nc.gpsimd.memset(identf[:, :], 0.0).then_inc(const_step, 1)
            nc.gpsimd.memset(identb[:, :], 0.0).then_inc(const_step, 1)
            nc.gpsimd.memset(causal[:, :], 0.0).then_inc(const_step, 1)
            nc.gpsimd.memset(chunkmask[:, :], 1).then_inc(const_step, 1)
            nc.gpsimd.memset(chunkcol[:, :], 1.0).then_inc(const_step, 1)
            nc.gpsimd.memset(scanmask[:, :], 1.0).then_inc(const_step, 1)
            nc.gpsimd.memset(mhalf[:, :], -0.5).then_inc(consts, 1)
            nc.gpsimd.memset(epsb[:, :], EPS).then_inc(consts, 1)
            pool.wait_ge(const_step, 6)
            for m in (identf, identb):
                nc.gpsimd.affine_select(out=m[:, :], in_=m[:, :], compare_op=ALU.not_equal, fill=1.0, base=0,
                                        pattern=[[-1, P]], channel_multiplier=1).then_inc(consts, 1)
            nc.gpsimd.affine_select(out=causal[:, :], in_=causal[:, :], compare_op=ALU.is_ge, fill=-1e30, base=0,
                                    pattern=[[-1, P]], channel_multiplier=1).then_inc(consts, 1)
            nc.gpsimd.affine_select(out=chunkmask[:, :], in_=chunkmask[:, :], compare_op=ALU.is_ge, fill=0, base=0,
                                    pattern=[[1, P]], channel_multiplier=-1).then_inc(const_step, 1)
            nc.gpsimd.affine_select(out=chunkcol[:, :], in_=chunkcol[:, :], compare_op=ALU.is_ge, fill=0.0, base=0,
                                    pattern=[[-CHUNK, CPT]], channel_multiplier=1).then_inc(const_step, 1)
            nc.gpsimd.memset(scanmask[:, :].rearrange("p (n j) -> p n j", j=CHUNK)[:, :, 0:1], 0.0).then_inc(consts, 1)
            pool.wait_ge(const_step, 8)
            nc.gpsimd.affine_select(out=chunkmask[:, :], in_=chunkmask[:, :], compare_op=ALU.is_ge, fill=0, base=0,
                                    pattern=[[-CHUNK, CPT], [0, CHUNK]], channel_multiplier=1).then_inc(consts, 1)
            nc.gpsimd.affine_select(out=chunkcol[:, :], in_=chunkcol[:, :], compare_op=ALU.is_ge, fill=0.0,
                                    base=CHUNK - 1, pattern=[[CHUNK, CPT]], channel_multiplier=-1).then_inc(consts, 1)

            root(pool, 0, ST)

            for p in range(HP):
                pool.wait_ge(he_done, 4 * p + 4)
                pool.wait_ge(hf_done, 2 * p + 2)
                pool.wait_ge(proj_out, 9)
                nc.gpsimd.tensor_tensor(he3[:, p], he3[:, p], hk[:, p], ALU.mult).then_inc(hprod, 1)
                nc.gpsimd.tensor_tensor(he2[:, p], he2[:, p], hk[:, p], ALU.mult).then_inc(hprod, 1)
                nc.gpsimd.tensor_tensor(he1[:, p], he1[:, p], hqT[:, p], ALU.mult).then_inc(hprod, 1)
                pool.wait_ge(hprod, 4 * p + 3)
                nc.gpsimd.tensor_tensor(hqT[:, p], hqT[:, p], he4[:, p], ALU.mult).then_inc(hprod, 1)
            pool.wait_ge(hprod, 4 * HP)
            pool.wait_ge(proj_out, 13)
            for p in range(HP):
                for t in range(ST):
                    i = p * ST + t
                    if i >= 2:
                        pool.wait_ge(u_done, i - 1)
                    for a in range(2):
                        h = 2 * p + a
                        vsrc = hv[:, t, h * HD:(h + 1) * HD].rearrange("p (o v) -> p o v", o=1).to_broadcast([P, CPT, HD])
                        csrc = chunkcol[:, :].rearrange("p (n o) -> p n o", o=1).to_broadcast([P, CPT, HD])
                        nc.gpsimd.tensor_tensor(vexp[i % 2][:, a], vsrc, csrc, ALU.mult).then_inc(vexp_done, 1)

            for h in range(FH):
                pool.wait_ge(f_ms, h + 1)
                nc.gpsimd.tensor_tensor(frstd[:, 4 * h:4 * h + 4], fss[:, 4 * h:4 * h + 4], mhalf[:, 0:4],
                                        ALU.pow).then_inc(f_rstd, 1)
            pool.wait_ge(ho_ps, 2)
            nc.gpsimd.iota(ranks, pattern=[[1, P]], base=0, channel_multiplier=0,
                               allow_small_or_imprecise_dtypes=True).then_inc(router_const, 1)
            nc.gpsimd.iota(tokid, pattern=[[P, ST]], base=0, channel_multiplier=1,
                               allow_small_or_imprecise_dtypes=True).then_inc(router_const, 1)
            nc.gpsimd.iota(ebase, pattern=[[P, EX]], base=0, channel_multiplier=0,
                               allow_small_or_imprecise_dtypes=True).then_inc(router_const, 1)
            nc.gpsimd.memset(before, 1.0).then_inc(router_step, 1)
            nc.gpsimd.memset(lower, 1.0).then_inc(router_step, 1)
            nc.gpsimd.memset(onesb, 1.0).then_inc(router_const, 1)
            pool.wait_ge(router_step, 2)
            nc.gpsimd.affine_select(out=before, in_=before, compare_op=ALU.is_gt, fill=0.0, base=0,
                                    pattern=[[1, P]], channel_multiplier=-1).then_inc(router_const, 1)
            nc.gpsimd.affine_select(out=lower, in_=lower, compare_op=ALU.is_gt, fill=0.0, base=0,
                                    pattern=[[1, 4], [-1, 4]], channel_multiplier=0).then_inc(router_const, 1)
            root(pool, 1, MT)
            root(pool, 2, ST)
            if STAGE == 3:
                experts_gathers(pool)

        def squares(act, stage, src, tiles):
            for t in range(tiles):
                nc.scalar.activation(n_sb[:, t, :], src[:, t, :], ACT.Square, accum_out=ss[:, t:t + 1]).then_inc(sq_done, 1)

        def turn_evac(eng, cnt, stage, dst, r0, width, which):
            for c in range(which, DC, 2):
                g = stage * DC + c
                eng.wait_ge(turned, g + 1)
                if which == 0:
                    nc.scalar.activation(dst[:, c, :], PS[4 + c % 4][:, 0:width], ACT.Copy,
                                         scale=pc[:, r0 + c:r0 + c + 1]).then_inc(cnt, 1)
                else:
                    nc.vector.tensor_scalar(dst[:, c, :], PS[4 + c % 4][:, 0:width], pc[:, r0 + c:r0 + c + 1], None,
                                            ALU.mult).then_inc(cnt, 1)

        def experts_act(act):
            act.wait_ge(x1_done, 16)
            act.wait_ge(n_done, 2 * ST + MT)
            squares(act, 3, x_sb, ST)
            turn_evac(act, turn_act, 3, hT, R_FFN, S, 0)
            act.wait_ge(soft_in, 1)
            nc.scalar.activation(gexp, gexp, ACT.Exp).then_inc(soft_out, 1)
            act.wait_ge(soft_in, 2)
            nc.scalar.activation(eexp, eexp, ACT.Exp).then_inc(soft_out, 1)

            def silu(e, b, first):
                act.wait_ge(gu_ps, e + 1)
                if not first:
                    act.wait_ge(hid_done, e - 1)
                nc.scalar.activation(sg[:, b], PS[2 + b][:, 0:FF], ACT.Silu).then_inc(silu_done, 1)

            def turned_hid(e, b, first):
                act.wait_ge(ht_ps, e + 1)
                if not first:
                    act.wait_ge(y_ps, 2 * (e - 1))
                nc.scalar.activation(hidT[:, b], PS[4][:, 0:2 * P].rearrange("p (k t) -> p k t", k=2), ACT.Copy).then_inc(ht_sb, 1)

            def y_half(e, b, first):
                act.wait_ge(y_ps, 2 * e + 1)
                if not first:
                    act.wait_ge(y_stored[b], 16 * ((e + (-b)) // 2))
                nc.scalar.activation(ysb[:, b, 0:512], PS[5][:, :], ACT.Copy).then_inc(y_act, 1)

            def step(e, j, start):
                if e is None or start is None or not (start and j == 0):
                    turned_hid(e - 1, (j + 1) % 2, start and j < 3)
                silu(e, j % 2, start and j < 2)
                if not (start and j == 0):
                    y_half(e - 1, (j + 1) % 2, start and j < 3)

            for j in range(SLOTS):
                step(j, j, True)
            with act.Fori(1, EX // SLOTS) as i:
                for j in range(SLOTS):
                    step(i * SLOTS + j, j, False)
            turned_hid(EX - 1, 1, False)
            y_half(EX - 1, 1, False)

            act.wait_ge(over_done, 1)
            with act.If(act.value_load(over[0:1, 0:1]) > 0):
                act.wait_ge(y_stored[0], 16 * EX // 2)
                act.wait_ge(y_stored[1], 16 * EX // 2)
                with act.Fori(0, (ST - 1) * EX) as k:
                    act.wait_ge(ov_gu, k + 1)
                    nc.scalar.activation(sg[:, 0], PS[2][:, 0:FF], ACT.Silu).then_inc(ov_silu, 1)
                    act.wait_ge(ov_ht_ps, k + 1)
                    nc.scalar.activation(hidT[:, 0], PS[4][:, 0:2 * P].rearrange("p (k t) -> p k t", k=2), ACT.Copy).then_inc(ov_ht_sb, 1)
                    act.wait_ge(ov_y_ps, 2 * k + 2)
                    nc.scalar.activation(ysb[:, 0, 0:512], PS[5][:, :], ACT.Copy).then_inc(ov_y_sb, 1)
                    nc.scalar.activation(ysb[:, 0, 512:1024], PS[6][:, :], ACT.Copy).then_inc(ov_y_sb, 1)
                    act.wait_ge(ov_stored, 16 * k + 16)
            with act.Else():
                pass
            for t in range(ST):
                act.wait_ge(fin_sum, 2 * t + 2)
                nc.scalar.activation(n_sb[:, t, :], x_sb[:, t, :], ACT.Square, accum_out=ss[:, t:t + 1]).then_inc(fin_sq, 1)

        PROJ = ([("t", cuT[:, c], ACT.Copy) for c in range(2)] + [("t", cgT[:, c], ACT.Sigmoid) for c in range(2)]
                + [("ff", lfa[:, :], ACT.Copy)]
                + [("t", hqT[:, c], ACT.Copy) for c in range(2)] + [("t", hfT[:, c], ACT.Sigmoid) for c in range(2)]
                + [("n", hv[:, t], ACT.Copy) for t in range(ST)] + [("t", hgT[:, c], ACT.Silu) for c in range(2)]
                + [("q", qT[:, c], ACT.Copy) for c in range(4)] + [("t", kT[:, c], ACT.Copy) for c in range(4)]
                + [("n", v[:, t], ACT.Copy) for t in range(ST)])

        @block.scalar
        def _(act):
            pr = [(mix_norm_g, R_MIX), (xatt_norm_g, R_XATT), (None, R_MEM), (ffn_norm_g, R_FFN), (fox_norm_g, R_FOX),
                  (hgrn_norm_g, R_HG), (hgrn_lb_logits, R_LB), (conv_b, R_CB), (conv_norm_g, R_CNG), (conv_norm_b, R_CNB)]
            for src, r in pr:
                row = mem_norm_g if src is None else src[0]
                k = row.shape[0] // P
                act.dma_start(prow[r:r + k, :], row.rearrange("(c p) -> c p", p=P)).then_inc(params_in, 16)
            act.dma_start(prow[R_CW:NR, :], conv_w[0].rearrange("w (c p) -> (w c) p", p=P)).then_inc(params_in, 16)
            act.dma_start(fbias[:, :], fox_f_bias[0].rearrange("(h o) -> h o", o=1)).then_inc(params_in, 16)
            act.dma_start(wff[:, :, :], win[:, :, C_FF:C_FF + FH]).then_inc(params_in, 16)

            act.wait_ge(x_in, 16)
            squares(act, 0, x_sb, ST)
            act.wait_ge(pcol, 1)
            turn_evac(act, turn_act, 0, hT, R_MIX, S, 0)

            def proj_evac(g0, g1):
                for g in range(g0, g1):
                    kind, dst, fn = PROJ[g]
                    act.wait_ge(proj, g + 1)
                    if kind == "ff":
                        nc.scalar.activation(dst, PS[g % 4][0:FH, :], ACT.Copy).then_inc(proj_out, 1)
                    elif kind == "q":
                        nc.scalar.activation(dst, PS[g % 4][:, :], fn, scale=FD ** -0.5).then_inc(proj_out, 1)
                    else:
                        w = dst.shape[-1]
                        nc.scalar.activation(dst, PS[g % 4][:, 0:w], fn).then_inc(proj_out, 1)

            proj_evac(0, 9)
            for p in range(HP):
                act.wait_ge(hf_done, 2 * p + 1)
                nc.scalar.activation(hgl[:, p], hfT[:, p], ACT.Ln).then_inc(hg_log, 1)
            act.wait_ge(lf_dve, 3)
            nc.scalar.activation(lfb[:, :], lfb[:, :], ACT.Exp, scale=-1.0).then_inc(lf_act, 1)
            act.wait_ge(lf_act, 1)
            nc.scalar.activation(lfb[:, :], lfb[:, :], ACT.Ln, bias=1.0).then_inc(lf_act, 1)
            proj_evac(9, 13)
            for p in range(HP):
                act.wait_ge(hd_done, 2 * p + 1)
                nc.scalar.activation(he1[:, p], hd1[:, p], ACT.Exp).then_inc(he_done, 1)
                nc.scalar.activation(he2[:, p], hd1[:, p], ACT.Exp, scale=-1.0).then_inc(he_done, 1)
                act.wait_ge(hd_done, 2 * p + 2)
                nc.scalar.activation(he3[:, p], hgl[:, p], ACT.Exp, scale=-1.0).then_inc(he_done, 1)
                nc.scalar.activation(he4[:, p], hb[:, p], ACT.Exp).then_inc(he_done, 1)
            proj_evac(13, 19)
            for p in range(HP):
                act.wait_ge(kh_turned, p + 1)
                nc.scalar.activation(khtok[:, p], PS[4 + p][:, :].rearrange("p (t k) -> p t k", t=ST), ACT.Copy).then_inc(kh_out, 1)
            proj_evac(19, 27)

            def inv_root(src, dst, done):
                nc.scalar.activation(dst, src, ACT.Ln, bias=epsb[:, 0:1]).then_inc(crs_step[0], 1)
                crs_step[1] += 1
                act.wait_ge(crs_step[0], crs_step[1])
                nc.scalar.activation(dst, dst, ACT.Exp, scale=-0.5).then_inc(done, 1)

            crs_step = [ctx_root, 0]
            act.wait_ge(consts, 2)
            for c in range(2):
                act.wait_ge(cvar, c + 1)
                inv_root(PS[6][:, :] if c == 0 else PS[7][:, :], croot[c], crs)
            for c in range(2):
                act.wait_ge(cz, c + 1)
                nc.scalar.activation(catT[:, 6 + c], cuT[:, c], ACT.Silu, bias=pc[:, R_CNB + c:R_CNB + c + 1],
                                     scale=pc[:, R_CNG + c:R_CNG + c + 1]).then_inc(co_done, 1)
            for p in range(HP):
                act.wait_ge(ho_ps, p + 1)
                nc.scalar.activation(hob[p], PS[4 + p][:, :], ACT.Copy).then_inc(ho_sb, 1)
            for p in range(HP):
                act.wait_ge(ho_ms, p + 1)
                inv_root(PS[6 + p][:, :], hrb[p], ho_rs)

            def f_exp(u):
                h, i = divmod(u, ST)
                act.wait_ge(m_done, u + 1)
                w = P * (i + 1)
                nc.scalar.activation(fs[u % 2][:, 0:w], fs[u % 2][:, 0:w], ACT.Exp, bias=fnm[:, u:u + 1],
                                     accum_out=frs[:, u:u + 1]).then_inc(p_done, 1)

            def f_pt(u):
                w = P * (u % ST + 1)
                act.wait_ge(pt_ps, u + 1)
                if u >= 2:
                    act.wait_ge(o_ps, u - 1)
                nc.scalar.activation(fpT[u % 2][:, 0:w], PS[2 + u % 2][:, 0:w], ACT.Copy).then_inc(pt_act, 1)

            for u in range(FH * ST + 1):
                if u < FH * ST:
                    f_exp(u)
                if u >= 1 and (u - 1) % 2 == 1:
                    f_pt(u - 1)

            act.wait_ge(mem_in, 16)
            act.wait_ge(wout_ps, 8)
            squares(act, 1, mem_sb, MT)
            turn_evac(act, turn_act, 1, memT, R_MEM, M, 0)
            act.wait_ge(x1_done, 8)
            act.wait_ge(turned, 2 * DC)
            act.wait_ge(n_done, ST + MT)
            squares(act, 2, x_sb, ST)

            def evac_n(base, dsts, cnt):
                for i, d in enumerate(dsts):
                    g = base + i
                    act.wait_ge(proj, g + 1)
                    nc.scalar.activation(d, PS[g % 4][:, 0:d.shape[-1]], ACT.Copy).then_inc(cnt, 1)

            evac_n(27, [xkT[:, c] for c in range(DC)] + [xv[:, t, 512 * n:512 * n + 512] for n in range(2) for t in range(MT)], proj_out)
            turn_evac(act, turn_act, 2, hT, R_XATT, S, 0)
            evac_n(39, [xqT[:, c] for c in range(DC)], proj_out)

            def x_exp(u):
                act.wait_ge(xm_done, u + 1)
                nc.scalar.activation(xp[:, u % 4, :], PS[u % 2][:, 0:M], ACT.Exp, bias=fnm[:, u:u + 1],
                                     scale=(D // XH) ** -0.5, accum_out=frs[:, u:u + 1]).then_inc(xe_done, 1)

            def x_out(h):
                for n in range(2):
                    g = 2 * h + n
                    act.wait_ge(xo_ps, g + 1)
                    nc.scalar.activation(xoT[:, g], PS[6 + n][:, :], ACT.Copy).then_inc(xo_sb, 1)

            for h in range(XH + 1):
                if h < XH:
                    for t in range(ST):
                        x_exp(h * ST + t)
                if h >= 1:
                    x_out(h - 1)
            if STAGE == 3:
                experts_act(act)

        def means(dve, stage, tiles, src, scale=1.0 / D):
            dve.wait_ge(sq_done, SQ[stage])
            nc.vector.tensor_scalar(ss[:, 0:tiles], ss[:, 0:tiles], scale, EPS, ALU.mult, ALU.add).then_inc(ms_done, 1)
            dve.wait_ge(rstd_done, stage + 1)
            for t in range(tiles):
                nc.vector.tensor_scalar(n_sb[:, t, :], src[:, t, :], rstd[:, t:t + 1], None, ALU.mult).then_inc(n_done, 1)

        SQ = [ST, ST + MT, 2 * ST + MT, 3 * ST + MT]

        def experts_dve(dve):
            means(dve, 3, ST, x_sb)
            turn_evac(dve, turn_dve, 3, hT, R_FFN, S, 1)

            steps = [0]

            def link(ins):
                steps[0] += 1
                ins.then_inc(route, 1)
                dve.wait_ge(route, steps[0])

            def over_last(ap, k):
                return ap.rearrange("p (a o) -> p a o", o=1).to_broadcast([P, ST, k])

            def across_rows(ap):
                return ap.rearrange("p t (o j) -> p t o j", o=1).to_broadcast([P, ST, 4, 4])

            def across_cols(ap):
                return ap.rearrange("p t (i o) -> p t i o", o=1).to_broadcast([P, ST, 4, 4])

            def rank(val, dst):
                link(nc.vector.tensor_tensor(beats, across_rows(val), across_cols(val), ALU.is_gt))
                link(nc.vector.tensor_tensor(ties, across_rows(val), across_cols(val), ALU.is_equal))
                low = lower.rearrange("p (o i) j -> p o i j", o=1).to_broadcast([P, ST, 4, 4])
                link(nc.vector.tensor_tensor(ties, ties, low, ALU.mult))
                link(nc.vector.tensor_tensor(beats, beats, ties, ALU.add))
                link(nc.vector.tensor_reduce(dst, beats, AX_X, ALU.add))

            dve.wait_ge(logits_ps, 1)
            dve.wait_ge(router_in, 16 * 4)
            dve.wait_ge(router_const, 6)
            link(nc.vector.tensor_tensor(logits, PS[0][:, 0:ST * (NG + EX)].rearrange("p (t n) -> p t n", t=ST),
                                         rbias.rearrange("p (o n) -> p o n", o=1).to_broadcast([P, ST, NG + EX]), ALU.add))
            gl = logits[:, :, 0:NG]
            el = logits[:, :, NG:].rearrange("p t (g e) -> p t g e", g=NG)
            link(nc.vector.tensor_reduce(gtop, gl, AX_X, ALU.max))
            nc.vector.tensor_tensor(gexp, gl, over_last(gtop, NG), ALU.subtract).then_inc(soft_in, 1)
            rank(gl, grank)
            link(nc.vector.tensor_scalar(ghot, grank, 0.0, None, ALU.is_equal))
            link(nc.vector.tensor_tensor(spread, el, across_cols(ghot), ALU.mult))
            link(nc.vector.tensor_reduce(esel, spread.rearrange("p t g e -> p t e g"), AX_X, ALU.add))
            link(nc.vector.tensor_reduce(etop, esel, AX_X, ALU.max))
            nc.vector.tensor_tensor(eexp, esel, over_last(etop, NE), ALU.subtract).then_inc(soft_in, 1)
            rank(esel, erank)
            link(nc.vector.tensor_scalar(ehot, erank, 2.0, None, ALU.is_lt))
            link(nc.vector.tensor_tensor(picked.rearrange("p t (g e) -> p t g e", g=NG), across_cols(ghot),
                                         across_rows(ehot), ALU.mult))
            nc.vector.tensor_copy(pickedb, picked).then_inc(picked_done, 1)
            dve.wait_ge(pos_ps, 1)
            link(nc.vector.tensor_copy(pos, PS[1][:, 0:ST * EX].rearrange("p (t e) -> p t e", t=ST)))
            link(nc.vector.scalar_tensor_tensor(out=posm, in0=picked, scalar=-4096.0, in1=pos, op0=ALU.mult, op1=ALU.add))
            link(nc.vector.tensor_scalar(posm, posm, 4096.0, None, ALU.add))
            for t in range(ST):
                nc.vector.tensor_tensor(pick[:, t], ranks.rearrange("p (o r) -> p o r", o=1).to_broadcast([P, EX, P]),
                                        posm[:, t].rearrange("p (e o) -> p e o", o=1).to_broadcast([P, EX, P]),
                                        ALU.is_equal).then_inc(pick_done, 1)
            dve.wait_ge(token_ps, 1)
            nc.vector.tensor_copy(token_of, PS[3][:, 0:EX]).then_inc(token_done, 1)
            link(nc.vector.tensor_reduce(most, PS[2][:, 0:EX], AX_X, ALU.max))
            nc.vector.tensor_scalar(over, most, float(P), None, ALU.is_gt).then_inc(over_done, 1)

            def combine():
                dve.wait_ge(soft_out, 1)
                link(nc.vector.tensor_reduce(gsum, gexp, AX_X, ALU.add))
                link(nc.vector.reciprocal(gsum, gsum))
                dve.wait_ge(soft_out, 2)
                link(nc.vector.tensor_tensor(eexp, eexp, ehot, ALU.mult))
                link(nc.vector.tensor_reduce(esum, eexp, AX_X, ALU.add))
                link(nc.vector.reciprocal(esum, esum))
                link(nc.vector.tensor_tensor(eexp, eexp, over_last(esum, NE), ALU.mult))
                link(nc.vector.tensor_tensor(eexp, eexp, over_last(gsum, NE), ALU.mult))
                link(nc.vector.tensor_tensor(weight.rearrange("p t (g e) -> p t g e", g=NG), across_cols(ghot),
                                             across_rows(eexp), ALU.mult))
                link(nc.vector.tensor_scalar(part, pos, float(P), None, ALU.is_ge))
                for k in range(2, ST):
                    link(nc.vector.scalar_tensor_tensor(out=part, in0=pos, scalar=float(k * P), in1=part, op0=ALU.is_ge, op1=ALU.add))
                link(nc.vector.scalar_tensor_tensor(out=slot, in0=part, scalar=float((EX - 1) * P), in1=pos, op0=ALU.mult, op1=ALU.add))
                link(nc.vector.tensor_tensor(slot, slot, ebase.rearrange("p (o e) -> p o e", o=1).to_broadcast([P, ST, EX]), ALU.add))
                link(nc.vector.tensor_tensor(slot, slot, picked, ALU.mult))
                link(nc.vector.tensor_reduce(stop_, slot, AX_X, ALU.max))
                link(nc.vector.tensor_reduce(ssum_, slot, AX_X, ALU.add))
                nc.vector.tensor_copy(slot2, stop_).then_inc(slots_done, 1)
                nc.vector.tensor_tensor(slot1, ssum_, stop_, ALU.subtract).then_inc(slots_done, 1)
                link(nc.vector.tensor_tensor(part, slot, over_last(stop_, EX), ALU.is_equal))
                link(nc.vector.tensor_tensor(part, part, weight, ALU.mult))
                link(nc.vector.tensor_reduce(w2nd, part, AX_X, ALU.add))
                link(nc.vector.tensor_tensor(part, slot, over_last(stop_, EX), ALU.not_equal))
                link(nc.vector.tensor_tensor(part, part, weight, ALU.mult))
                link(nc.vector.tensor_reduce(w1st, part, AX_X, ALU.add))

            gains = pc[:, R_FFN:R_FFN + DC]

            def turned_rows(e, b, first):
                if not first:
                    dve.wait_ge(gu_ps, e - 1)
                for k in range(2):
                    dve.wait_ge(xt_ps, 2 * e + k + 1)
                    nc.vector.tensor_tensor(xgT[:, b, 4 * k:4 * k + 4, :], PS[k][:, :].rearrange("p (c t) -> p c t", c=4),
                                            gains[:, 4 * k:4 * k + 4].rearrange("p (c o) -> p c o", o=1).to_broadcast([P, 4, P]),
                                            ALU.mult).then_inc(xt_sb, 1)

            def hidden(e, b, first):
                dve.wait_ge(silu_done, e + 1)
                if not first:
                    dve.wait_ge(ht_ps, e - 1)
                nc.vector.tensor_tensor(hid[:, b], sg[:, b], PS[2 + b][:, FF:2 * FF], ALU.mult).then_inc(hid_done, 1)

            def y_half(e, b, first):
                dve.wait_ge(y_ps, 2 * e + 2)
                if not first:
                    dve.wait_ge(y_stored[b], 16 * ((e + (-b)) // 2))
                nc.vector.tensor_copy(ysb[:, b, 512:1024], PS[6][:, :]).then_inc(y_dve, 1)

            def step(e, j, start):
                turned_rows(e, j % 2, start and j < 2)
                hidden(e, j % 2, start and j < 2)
                if not (start and j == 0):
                    y_half(e - 1, (j + 1) % 2, start and j < 3)
                if start and j == 0:
                    combine()

            for j in range(SLOTS):
                step(j, j, True)
            with dve.Fori(1, EX // SLOTS) as i:
                for j in range(SLOTS):
                    step(i * SLOTS + j, j, False)
            y_half(EX - 1, 1, False)

            with dve.If(dve.value_load(over[0:1, 0:1]) > 0):
                dve.wait_ge(gu_ps, EX)
                dve.wait_ge(ht_ps, EX)
                with dve.Fori(0, ST - 1) as q:
                    nc.vector.tensor_scalar(posm, posm, -float(P), None, ALU.add).then_inc(ov_pos, 1)
                    with dve.Fori(0, EX) as e:
                        k = q * EX + e
                        dve.wait_ge(ov_pos, q + 1)
                        for t in range(ST):
                            nc.vector.tensor_scalar(ov_pick[:, t], ranks, posm[:, t, bass.ds(e, 1)], None,
                                                    ALU.is_equal).then_inc(ov_picked, 1)
                        dve.wait_ge(ov_token_ps, k + 1)
                        nc.vector.tensor_copy(ov_token, PS[3][:, 0:1]).then_inc(ov_token_sb, 1)
                        for n in range(2):
                            dve.wait_ge(ov_xt_ps, 2 * k + n + 1)
                            nc.vector.tensor_tensor(xgT[:, 0, 4 * n:4 * n + 4, :], PS[n][:, :].rearrange("p (c t) -> p c t", c=4),
                                                    gains[:, 4 * n:4 * n + 4].rearrange("p (c o) -> p c o", o=1).to_broadcast([P, 4, P]),
                                                    ALU.mult).then_inc(ov_xt_sb, 1)
                        dve.wait_ge(ov_silu, k + 1)
                        nc.vector.tensor_tensor(hid[:, 0], sg[:, 0], PS[2][:, FF:2 * FF], ALU.mult).then_inc(ov_hid, 1)
                        dve.wait_ge(ov_stored, 16 * k + 16)
            with dve.Else():
                pass
            for t in range(ST + 1):
                if t < ST:
                    dve.wait_ge(fin_in[t % 2], 32 * (t // 2 + 1))
                    for k, w in enumerate((w1st, w2nd)):
                        if k:
                            dve.wait_ge(fin_sum, 2 * t + 1)
                        nc.vector.scalar_tensor_tensor(out=x_sb[:, t, :], in0=ygath[:, t % 2, k, :], scalar=w[:, t:t + 1],
                                                       in1=x_sb[:, t, :], op0=ALU.mult, op1=ALU.add).then_inc(fin_sum, 1)
                if t >= 1:
                    u = t - 1
                    dve.wait_ge(fin_root, u + 1)
                    if u == 0:
                        dve.wait_ge(router_in, 16 * 5)
                        dve.wait_ge(n_stored, 16)
                    nc.vector.scalar_tensor_tensor(out=n_sb[:, u, :], in0=x_sb[:, u, :], scalar=rstd[:, u:u + 1],
                                                   in1=fgain, op0=ALU.mult, op1=ALU.mult).then_inc(fin_out, 1)
                if t < ST:
                    dve.wait_ge(fin_sq, t + 1)
                    nc.vector.tensor_scalar(ss[:, t:t + 1], ss[:, t:t + 1], 1.0 / D, EPS, ALU.mult, ALU.add).then_inc(fin_ms, 1)
        @block.vector
        def _(dve):
            nc.vector.memset(half64[:, :], 0.0).then_inc(half_done, 1)
            dve.wait_ge(half_done, 1)
            nc.vector.memset(half64[0:64, 0:64], 1.0 / 64).then_inc(half_done, 1)
            nc.vector.memset(half64[64:128, 64:128], 1.0 / 64).then_inc(half_done, 1)
            means(dve, 0, ST, x_sb)
            dve.wait_ge(pcol_ps, 1)
            nc.vector.tensor_copy(pc[:, :], PS[0][:, 0:NR]).then_inc(pcol, 1)
            dve.wait_ge(pcol, 1)
            turn_evac(dve, turn_dve, 0, hT, R_MIX, S, 1)

            dve.wait_ge(pcol, 1)
            lg = pc[:, R_LB:R_LB + HP]
            nc.vector.tensor_tensor(lbv[:, 0:2], lg, lg, ALU.subtract).then_inc(lb_step, 1)
            dve.wait_ge(lb_step, 1)
            nc.vector.tensor_tensor(lbv[:, 2:4], lbv[:, 0:2], lbv[:, 0:2], ALU.subtract).then_inc(lb_step, 1)
            dve.wait_ge(lb_step, 2)
            nc.vector.tensor_scalar(lbv[:, 4:6], lbv[:, 2:4], -1.0, 1.0, ALU.mult, ALU.add).then_inc(lb_step, 1)

            for c in range(2):
                dve.wait_ge(proj_out, 3 + c)
                nc.vector.tensor_tensor(cuT[:, c], cuT[:, c], cgT[:, c], ALU.mult).then_inc(conv_a, 1)
            dve.wait_ge(proj_out, 5)
            nc.vector.memset(ones8[:, :], 1.0).then_inc(ones_done, 1)
            nc.vector.tensor_scalar(lfa[:, :], lfa[:, :], fbias[:, 0:1], None, ALU.add).then_inc(lf_dve, 1)
            dve.wait_ge(lf_dve, 1)
            nc.vector.scalar_tensor_tensor(out=lfb[:, :], in0=lfa[:, :], scalar=-1.0, in1=lfa[:, :], op0=ALU.mult,
                                           op1=ALU.max).then_inc(lf_dve, 1)
            dve.wait_ge(lf_dve, 2)
            nc.vector.tensor_scalar(lfa[:, :], lfa[:, :], 0.0, None, ALU.min).then_inc(lf_dve, 1)
            dve.wait_ge(lb_step, 3)
            for p in range(HP):
                dve.wait_ge(proj_out, 8 + p)
                nc.vector.tensor_scalar(hfT[:, p], hfT[:, p], lbv[:, 4 + p:5 + p], lbv[:, 2 + p:3 + p], ALU.mult,
                                        ALU.add).then_inc(hf_done, 1)
                dve.wait_ge(hf_done, 2 * p + 1)
                nc.vector.tensor_scalar(hk[:, p], hfT[:, p], -1.0, 1.0, ALU.mult, ALU.add).then_inc(hf_done, 1)

            def conv(c, w0, w1):
                y, a = cgT[:, c], cuT[:, c]
                for w in range(w0, w1):
                    s = w
                    r = R_CW + 2 * (CW - 1 - s) + c
                    if s == 0:
                        dve.wait_ge(conv_a, c + 1)
                        nc.vector.tensor_scalar(y, a, pc[:, r:r + 1], pc[:, R_CB + c:R_CB + c + 1], ALU.mult,
                                                ALU.add).then_inc(conv_y, 1)
                    else:
                        dve.wait_ge(conv_y, c * CW + s)
                        nc.vector.scalar_tensor_tensor(out=y[:, s:S], in0=a[:, 0:S - s], scalar=pc[:, r:r + 1],
                                                       in1=y[:, s:S], op0=ALU.mult, op1=ALU.add).then_inc(conv_y, 1)

            for p in range(HP):
                dve.wait_ge(hg_log, p + 1)
                if p == 0:
                    dve.wait_ge(consts, 8)
                nc.vector.tensor_tensor_scan(hb[:, p], scanmask[:, :], hgl[:, p], 0.0, ALU.mult, ALU.add).then_inc(hb_done, 1)
                dve.wait_ge(hb_done, p + 1)
                b3 = hb[:, p].rearrange("p (n j) -> p n j", j=CHUNK)
                nc.vector.tensor_tensor(hd1[:, p].rearrange("p (n j) -> p n j", j=CHUNK), b3,
                                        b3[:, :, CHUNK // 2:CHUNK // 2 + 1].to_broadcast([P, NCH, CHUNK]),
                                        ALU.subtract).then_inc(hd_done, 1)
                nc.vector.tensor_tensor(hgl[:, p].rearrange("p (n j) -> p n j", j=CHUNK), b3,
                                        b3[:, :, CHUNK - 1:CHUNK].to_broadcast([P, NCH, CHUNK]),
                                        ALU.subtract).then_inc(hd_done, 1)
            dve.wait_ge(lf_act, 2)
            nc.vector.tensor_tensor(lfb[:, :], lfb[:, :], lfa[:, :], ALU.subtract).then_inc(lf_dve, 1)
            dve.wait_ge(lf_dve, 4)
            dve.wait_ge(ones_done, 1)
            nc.vector.tensor_tensor_scan(lfa[:, :], ones8[:, :], lfb[:, :], 0.0, ALU.mult, ALU.add).then_inc(lf_dve, 1)

            conv(0, 0, CW)
            conv(1, 0, CW)
            dve.wait_ge(he_done, 4 * HP)
            nc.vector.memset(attm.rearrange("p a b c -> p (a b c)"), 0.0).then_inc(att_zero, 1)
            for c in range(2):
                dve.wait_ge(cmean, c + 1)
                nc.vector.tensor_tensor(cuT[:, c], cgT[:, c], PS[6 + c][:, :], ALU.subtract).then_inc(cdev, 1)
                dve.wait_ge(cdev, 2 * c + 1)
                nc.vector.tensor_tensor(cgT[:, c], cuT[:, c], cuT[:, c], ALU.mult).then_inc(cdev, 1)

            nc.vector.memset(states[:, 0, :], 0.0).then_inc(state_step, 1)
            n_state = 1

            def states_of(p, n_state):
                for t in range(ST):
                    i = p * ST + t
                    dve.wait_ge(u_done, i + 1)
                    for n in range(CPT):
                        k = t * CPT + n
                        dve.wait_ge(state_step, n_state)
                        nc.vector.scalar_tensor_tensor(
                            out=states[:, k + 1, :], in0=states[:, k, :],
                            scalar=he4[:, p, k * CHUNK + CHUNK - 1:k * CHUNK + CHUNK],
                            in1=PS[i % 2][:, n * HD:(n + 1) * HD], op0=ALU.mult, op1=ALU.add).then_inc(state_step, 1)
                        n_state += 1
                return n_state

            def att_mask(p):
                for a in range(2):
                    h = 2 * p + a
                    dve.wait_ge(att_ps, h + 1)
                    nc.vector.copy_predicated(attm[:, h], chunkmask[:, :].rearrange("p (o t) -> p o t", o=1).to_broadcast([P, ST, P]),
                                              PS[2 + a][:, :].rearrange("p (t s) -> p t s", t=ST)).then_inc(att_done, 1)

            dve.wait_ge(att_zero, 1)
            att_mask(0)
            n_state = states_of(0, n_state)
            att_mask(1)
            dve.wait_ge(ho_ps, 1)
            n_state = states_of(1, n_state)

            for c in range(2):
                dve.wait_ge(crs, c + 1)
                nc.vector.tensor_tensor(cuT[:, c], cuT[:, c], croot[c], ALU.mult).then_inc(cz, 1)
            for p in range(HP):
                dve.wait_ge(ho_sb, p + 1)
                nc.vector.tensor_tensor(he3[:, p], hob[p], hob[p], ALU.mult).then_inc(ho_sq, 1)
            for p in range(HP):
                dve.wait_ge(ho_rs, p + 1)
                nc.vector.scalar_tensor_tensor(out=hob[p], in0=hob[p], scalar=pc[:, R_HG + p:R_HG + p + 1],
                                               in1=hrb[p], op0=ALU.mult, op1=ALU.mult).then_inc(ho_step, 1)
                dve.wait_ge(ho_step, 2 * p + 1)
                nc.vector.tensor_tensor(catT[:, 4 + p], hob[p], hgT[:, p], ALU.mult).then_inc(ho_step, 1)

            def f_scores(u):
                h, i = divmod(u, ST)
                w = P * (i + 1)
                if i == 0:
                    dve.wait_ge(negc_ps, h + 1)
                    nc.vector.tensor_copy(fnegc[h % 2], PS[6 + h % 2][:, :]).then_inc(negc_sb, 1)
                    dve.wait_ge(negc_sb, h + 1)
                dve.wait_ge(qk_done, u + 1)
                if u >= 2:
                    dve.wait_ge(pt_ps, u - 1)
                nc.vector.tensor_tensor_reduce(fs[u % 2][:, 0:w], PS[u % 2][:, 0:w], fnegc[h % 2][:, 0:w], 1.0, LOWEST,
                                               ALU.add, ALU.max, fmx[:, u:u + 1]).then_inc(s_done, 1)
                dve.wait_ge(s_done, u + 1)
                nc.vector.tensor_scalar(fnm[:, u:u + 1], fmx[:, u:u + 1], -1.0, None, ALU.mult).then_inc(m_done, 1)

            def f_pt(u):
                w = P * (u % ST + 1)
                dve.wait_ge(pt_ps, u + 1)
                if u >= 2:
                    dve.wait_ge(o_ps, u - 1)
                nc.vector.tensor_copy(fpT[u % 2][:, 0:w], PS[2 + u % 2][:, 0:w]).then_inc(pt_dve, 1)

            def f_out(u):
                h, i = divmod(u, ST)
                dve.wait_ge(p_done, u + 1)
                nc.vector.reciprocal(frr[:, u:u + 1], frs[:, u:u + 1]).then_inc(f_step, 1)
                dve.wait_ge(f_step, u + 1)
                dve.wait_ge(o_ps, u + 1)
                nc.vector.tensor_scalar(fo[:, i, h * FD:(h + 1) * FD], PS[4 + u % 2][:, 0:FD], frr[:, u:u + 1], None,
                                        ALU.mult).then_inc(o_sb, 1)

            k_f = 0

            def f_square(h, k_f):
                dve.wait_ge(o_sb, ST * (h + 1))
                if h:
                    dve.wait_ge(f_ms, h)
                src = fo[:, :, h * FD:(h + 1) * FD]
                nc.vector.tensor_tensor(fsq, src, src, ALU.mult).then_inc(fsteps, 1)
                dve.wait_ge(fsteps, k_f + 1)
                nc.vector.tensor_reduce(fss[:, 4 * h:4 * h + 4], fsq, AX_X, ALU.add).then_inc(fsteps, 1)
                dve.wait_ge(fsteps, k_f + 2)
                nc.vector.tensor_scalar(fss[:, 4 * h:4 * h + 4], fss[:, 4 * h:4 * h + 4], 1.0 / FD, EPS, ALU.mult,
                                        ALU.add).then_inc(f_ms, 1)
                return k_f + 2

            def f_norm(h):
                dve.wait_ge(f_rstd, h + 1)
                src = fo[:, :, h * FD:(h + 1) * FD]
                nc.vector.tensor_tensor(src, src, frstd[:, 4 * h:4 * h + 4].rearrange("p (t o) -> p t o", o=1).to_broadcast([P, ST, FD]),
                                        ALU.mult).then_inc(fnorm, 1)

            fnorm = f_normed
            for u in range(FH * ST + 2):
                if u < FH * ST:
                    f_scores(u)
                if 1 <= u <= FH * ST and (u - 1) % 2 == 0:
                    f_pt(u - 1)
                if u >= 2:
                    f_out(u - 2)
                    if (u - 2) % ST == ST - 1:
                        h = (u - 2) // ST
                        k_f = f_square(h, k_f)
                        if h >= 1:
                            f_norm(h - 1)
            f_norm(FH - 1)
            for c in range(4):
                dve.wait_ge(fo_turned, c + 1)
                nc.vector.tensor_scalar(catT[:, c], PS[6 + c % 2][:, :], pc[:, R_FOX + c:R_FOX + c + 1], None,
                                        ALU.mult).then_inc(cat_out, 1)

            def residual(base):
                for g in range(8):
                    t, n = divmod(g, 2)
                    dve.wait_ge(wout_ps, base + g + 1)
                    xs = x_sb[:, t, 512 * n:512 * n + 512]
                    nc.vector.tensor_tensor(xs, xs, PS[g % 4][:, :], ALU.add).then_inc(x1_done, 1)

            residual(0)
            means(dve, 1, MT, mem_sb)
            turn_evac(dve, turn_dve, 1, memT, R_MEM, M, 1)
            means(dve, 2, ST, x_sb)
            turn_evac(dve, turn_dve, 2, hT, R_XATT, S, 1)

            def x_max(u):
                dve.wait_ge(xs_ps, u + 1)
                nc.vector.tensor_reduce(fmx[:, u:u + 1], PS[u % 2][:, 0:M], AX_X, ALU.max).then_inc(xs_step, 1)
                dve.wait_ge(xs_step, u + 1)
                nc.vector.tensor_scalar(fnm[:, u:u + 1], fmx[:, u:u + 1], -((D // XH) ** -0.5), None,
                                        ALU.mult).then_inc(xm_done, 1)

            def x_norm(u):
                dve.wait_ge(xe_done, u + 1)
                nc.vector.reciprocal(frr[:, u:u + 1], frs[:, u:u + 1]).then_inc(xr_done, 1)
                dve.wait_ge(xr_done, u + 1)
                nc.vector.tensor_scalar(xp[:, u % 4, :], xp[:, u % 4, :], frr[:, u:u + 1], None, ALU.mult).then_inc(xn_done, 1)

            def x_pt(h):
                for m in range(2):
                    g = 2 * h + m
                    dve.wait_ge(xpt_ps, g + 1)
                    if h >= 2:
                        dve.wait_ge(xo_ps, 2 * (h - 1))
                    nc.vector.tensor_copy(xpT[:, g % 4], PS[4 + m][:, :]).then_inc(xpt_sb, 1)

            for h in range(XH + 1):
                if h < XH:
                    for t in range(ST):
                        x_max(h * ST + t)
                        if t >= 1:
                            x_norm(h * ST + t - 1)
                    x_norm(h * ST + ST - 1)
                    x_pt(h)
            if STAGE > 1:
                residual(8)
            if STAGE == 3:
                experts_dve(dve)

        def experts_pe(pe, turn):
            pe.wait_ge(xo_sb, 8)
            turn(3, ST, 2 * ST + MT)
            pe.wait_ge(turn_act, 16)
            pe.wait_ge(turn_dve, 16)
            pe.wait_ge(x1_done, 16)
            pe.wait_ge(router_in, 16 * 4)
            for t in range(ST):
                for c in range(DC):
                    mm = nc.tensor.matmul(PS[0][:, t * (NG + EX):(t + 1) * (NG + EX)], hT[:, c, t * P:(t + 1) * P],
                                          wgr[:, c, :], start=c == 0, stop=c == DC - 1)
            mm.then_inc(logits_ps, 1)
            pe.wait_ge(picked_done, 1)
            pe.wait_ge(router_const, 6)
            for t in range(ST):
                for u in range(t + 1):
                    nc.tensor.matmul(PS[1][:, t * EX:(t + 1) * EX], onesb if u < t else before, pickedb[:, u],
                                     start=u == 0, stop=u == t)
            for u in range(ST):
                mm = nc.tensor.matmul(PS[2][:, 0:EX], onesb, pickedb[:, u], start=u == 0, stop=u == ST - 1)
            mm.then_inc(pos_ps, 1)
            for t in range(ST):
                pe.wait_ge(pick_done, t + 1)
                for e in range(EX):
                    mm = nc.tensor.matmul(PS[3][:, e:e + 1], pick[:, t, e, :], tokid[:, t:t + 1], start=t == 0 and e == 0,
                                          stop=t == ST - 1 and e == EX - 1, skip_group_check=True)
            mm.then_inc(token_ps, 1)

            def turn_rows(src, b, done):
                for k in range(2):
                    for c in range(4):
                        mm = nc.tensor.transpose(PS[k][:, c * P:(c + 1) * P], src[:, b, (4 * k + c) * P:(4 * k + c + 1) * P], identf[:, :])
                    mm.then_inc(done, 1)

            def turn_hidden(b, done):
                for k in range(2):
                    mm = nc.tensor.transpose(PS[4][:, k * P:(k + 1) * P], hid[:, b, k * P:(k + 1) * P], identf[:, :])
                mm.then_inc(done, 1)

            def gate_up(b, s, bank, done):
                for c in range(DC):
                    mm = nc.tensor.matmul(bank[:, :], xgT[:, b, c, :], W[:, s, c, :], start=c == 0, stop=c == DC - 1)
                mm.then_inc(done, 1)

            def down(b, s, n, done):
                for k in range(2):
                    mm = nc.tensor.matmul(PS[5 + n][:, :], hidT[:, b, k, :], Dn[:, s, k, 512 * n:512 * n + 512],
                                          start=k == 0, stop=k == 1)
                mm.then_inc(done, 1)

            def step(e, j, turn_, start, last=False):
                b = j % 2
                if not last:
                    pe.wait_ge(xg_in[b], 16 * ((e + (2 - b)) // 2))
                    if not (start and j == 0):
                        pe.wait_ge(xt_sb, 2 * e)
                    elif start:
                        pe.wait_ge(over_done, 1)
                    turn_rows(xg, b, xt_ps)
                if not (start and j == 0):
                    pe.wait_ge(hid_done, e)
                    if not (start and j == 1):
                        pe.wait_ge(ht_sb, e - 1)
                    turn_hidden(1 - b, ht_ps)
                if not last:
                    pe.wait_ge(xt_sb, 2 * e + 2)
                    gate_up_loaded(pe, j, turn_)
                    gate_up(b, j, PS[2 + b], gu_ps)
                if not (start and j == 0):
                    s = (j - 1) % SLOTS
                    pe.wait_ge(ht_sb, e)
                    pe.wait_ge(dn_loaded[s], 16 * (turn_ + (0 if j == 0 else 1)))
                    for n, left in enumerate((y_act, y_dve)):
                        if not (start and j == 1):
                            pe.wait_ge(left, e - 1)
                        down(1 - b, s, n, y_ps)

            for j in range(SLOTS):
                step(j, j, 0, True)
            with pe.Fori(1, EX // SLOTS) as i:
                for j in range(SLOTS):
                    step(i * SLOTS + j, j, i, False)
            step(EX, 0, EX // SLOTS, False, last=True)

            pe.wait_ge(over_done, 1)
            with pe.If(pe.value_load(over[0:1, 0:1]) > 0):
                pe.wait_ge(y_act, EX)
                pe.wait_ge(y_dve, EX)
                with pe.Fori(0, (ST - 1) * EX) as k:
                    pe.wait_ge(ov_picked, ST * k + ST)
                    for t in range(ST):
                        mm = nc.tensor.matmul(PS[3][:, 0:1], ov_pick[:, t], tokid[:, t:t + 1], start=t == 0, stop=t == ST - 1)
                    mm.then_inc(ov_token_ps, 1)
                    pe.wait_ge(ov_xg, 16 * k + 16)
                    turn_rows(xg, 0, ov_xt_ps)
                    pe.wait_ge(ov_xt_sb, 2 * k + 2)
                    pe.wait_ge(ov_w, 48 * k + 48)
                    gate_up(0, 0, PS[2], ov_gu)
                    pe.wait_ge(ov_hid, k + 1)
                    turn_hidden(0, ov_ht_ps)
                    pe.wait_ge(ov_ht_sb, k + 1)
                    for n in range(2):
                        down(0, 0, n, ov_y_ps)
                    pe.wait_ge(ov_y_sb, 2 * k + 2)
            with pe.Else():
                pass

        @block.tensor
        def _(pe):
            pe.wait_ge(params_in, 13 * 16)
            pe.wait_ge(consts, 5)
            nc.tensor.transpose(PS[0][:, 0:NR], prow[0:NR, :], identf[0:NR, 0:NR]).then_inc(pcol_ps, 1)

            def turn(stage, tiles, n0):
                pe.wait_ge(n_done, n0 + tiles)
                for c in range(DC):
                    g = stage * DC + c
                    if g >= 4:
                        pe.wait_ge(turn_act if c % 2 == 0 else turn_dve, g // 2 - 1)
                    for t in range(tiles):
                        mm = nc.tensor.transpose(PS[4 + c % 4][:, t * P:(t + 1) * P], n_sb[:, t, c * P:(c + 1) * P], identf[:, :])
                    mm.then_inc(turned, 1)

            turn(0, ST, 0)
            pe.wait_ge(turn_act, 4)
            pe.wait_ge(turn_dve, 4)
            pe.wait_ge(pcol, 1)

            def across(slot, col, w=P, src=None, n=S):
                src = hT if src is None else src

                def f(bank):
                    for c in range(DC):
                        lhs = wff[:, c, :] if slot is None else W[:, slot, c, col:col + w]
                        mm = nc.tensor.matmul(bank[0:w, 0:n], lhs, src[:, c, 0:n], start=c == 0, stop=c == DC - 1)
                    return mm
                return f

            def along(slot, t, col, w, src=None):
                src = hT if src is None else src

                def f(bank):
                    for c in range(DC):
                        mm = nc.tensor.matmul(bank[:, 0:w], src[:, c, t * P:(t + 1) * P], W[:, slot, c, col:col + w],
                                              start=c == 0, stop=c == DC - 1)
                    return mm
                return f

            g = 0

            def run(fs_, g, n_load):
                loaded(pe, n_load)
                for k, f in enumerate(fs_):
                    if g >= 4:
                        pe.wait_ge(proj_out, g - 3)
                    mm = f(PS[g % 4])
                    mm.then_inc(proj, 1)
                    g += 1
                return g

            g = run([across(0, P * c) for c in range(4)], g, 0)
            g = run([across(None, 0, FH)], g, 0)
            g = run([across(1, P * c) for c in range(4)], g, 1)
            g = run([along(2, t, 0, HW) for t in range(ST)], g, 2)
            g = run([across(2, HW + P * c) for c in range(2)], g, 2)
            g = run([across(3, P * c) for c in range(4)], g, 3)

            for p in range(HP):
                pe.wait_ge(hprod, 4 * p + 1)
                for t in range(ST):
                    mm = nc.tensor.transpose(PS[4 + p][:, t * P:(t + 1) * P], he3[:, p, t * P:(t + 1) * P], identf[:, :])
                mm.then_inc(kh_turned, 1)
            g = run([across(0, P * c) for c in range(4)], g, 4)
            g = run([along(1, t, 0, FW) for t in range(ST)], g, 5)
            pe.wait_ge(half_done, 3)
            for c in range(2):
                pe.wait_ge(conv_y, CW * (c + 1))
                nc.tensor.matmul(PS[6 + c][:, :], half64[:, :], cgT[:, c], start=True, stop=True).then_inc(cmean, 1)
            for c in range(2):
                pe.wait_ge(cdev, 2 * c + 2)
                nc.tensor.matmul(PS[6 + c][:, :], half64[:, :], cgT[:, c], start=True, stop=True).then_inc(cvar, 1)

            pe.wait_ge(proj_out, 27)
            for p in range(HP):
                if p:
                    pe.wait_ge(att_done, 2)
                pe.wait_ge(hprod, 4 * p + 4)
                for a in range(2):
                    r = slice(64 * a, 64 * a + 64)
                    for t in range(ST):
                        mm = nc.tensor.matmul(PS[2 + a][:, t * P:(t + 1) * P], he2[r, p, t * P:(t + 1) * P],
                                              he1[r, p, t * P:(t + 1) * P], start=True, stop=True)
                    mm.then_inc(att_ps, 1)
                pe.wait_ge(kh_out, p + 1)
                for t in range(ST):
                    i = p * ST + t
                    pe.wait_ge(vexp_done, 2 * i + 2)
                    if i >= 2:
                        pe.wait_ge(state_step, 1 + CPT * (i - 1))
                    for a in range(2):
                        mm = nc.tensor.matmul(PS[i % 2][64 * a:64 * a + 64, :], khtok[:, p, t, 64 * a:64 * a + 64],
                                              vexp[i % 2][:, a].rearrange("p n v -> p (n v)"), start=True, stop=True)
                    mm.then_inc(u_done, 1)
                pe.wait_ge(att_done, 2 * p + 2)
                pe.wait_ge(state_step, 1 + CPT * ST * (p + 1) - 1)
                bank = PS[4 + p]
                for a in range(2):
                    h = 2 * p + a
                    r = slice(64 * a, 64 * a + 64)
                    for t in range(ST):
                        nc.tensor.matmul(bank[r, t * P:(t + 1) * P], hv[:, t, h * HD:(h + 1) * HD], attm[:, h, t, :],
                                         start=t == 0, stop=False, skip_group_check=True)
                    for n in range(NCH):
                        mm = nc.tensor.matmul(bank[r, n * CHUNK:(n + 1) * CHUNK], states[r, n, :],
                                              hqT[r, p, n * CHUNK:(n + 1) * CHUNK], start=False, stop=n == NCH - 1,
                                              skip_group_check=True)
                mm.then_inc(ho_ps, 1)
            pe.wait_ge(crs, 2)
            for p in range(HP):
                pe.wait_ge(ho_sq, p + 1)
                nc.tensor.matmul(PS[6 + p][:, :], half64[:, :], he3[:, p], start=True, stop=True).then_inc(ho_ms, 1)

            def negc(h):
                if h == 0:
                    pe.wait_ge(lf_dve, 5)
                    pe.wait_ge(ho_rs, 2)
                if h >= 2:
                    pe.wait_ge(negc_sb, h - 1)
                nc.tensor.matmul(PS[6 + h % 2][:, :], identf[0:FH, h:h + 1].to_broadcast([FH, P]), lfa[:, :],
                                 start=True, stop=True).then_inc(negc_ps, 1)

            def qk(u):
                h, i = divmod(u, ST)
                r = slice(64 * (h % 2), 64 * (h % 2) + 64)
                if u >= 2:
                    pe.wait_ge(s_done, u - 1)
                nc.tensor.matmul(PS[u % 2][:, 0:P * (i + 1)], qT[r, h // 2, i * P:(i + 1) * P],
                                 kT[r, h // 2, 0:P * (i + 1)], start=True, stop=False)
                nc.tensor.matmul(PS[u % 2][:, P * i:P * (i + 1)], identb[:, :], causal[:, :], start=False,
                                 stop=True).then_inc(qk_done, 1)

            def pt(u):
                i = u % ST
                pe.wait_ge(p_done, u + 1)
                if u >= 2:
                    pe.wait_ge(pt_dve if u % 2 == 0 else pt_act, u // 2)
                for j in range(i + 1):
                    mm = nc.tensor.transpose(PS[2 + u % 2][:, j * P:(j + 1) * P], fs[u % 2][:, j * P:(j + 1) * P], identf[:, :])
                mm.then_inc(pt_ps, 1)

            def pv(u):
                h, i = divmod(u, ST)
                pe.wait_ge(pt_dve if u % 2 == 0 else pt_act, u // 2 + 1)
                if u >= 2:
                    pe.wait_ge(o_sb, u - 1)
                for j in range(i + 1):
                    mm = nc.tensor.matmul(PS[4 + u % 2][:, 0:FD], fpT[u % 2][:, j * P:(j + 1) * P],
                                          v[:, j, h * FD:(h + 1) * FD], start=j == 0, stop=j == i)
                mm.then_inc(o_ps, 1)

            pe.wait_ge(consts, 5)
            pe.wait_ge(att_done, 4)
            pe.wait_ge(state_step, 1 + HP * NCH)
            pe.wait_ge(ho_sb, 2)
            negc(0)
            negc(1)
            for u in range(FH * ST + 2):
                if u < FH * ST:
                    qk(u)
                if u % ST == 1 and 2 <= u // ST + 1 < FH:
                    negc(u // ST + 1)
                if 1 <= u <= FH * ST:
                    pt(u - 1)
                if u >= 2:
                    pv(u - 2)
            pe.wait_ge(negc_sb, FH)
            for c in range(4):
                pe.wait_ge(f_normed, 2 * c + 2)
                if c >= 2:
                    pe.wait_ge(cat_out, c - 1)
                for t in range(ST):
                    mm = nc.tensor.transpose(PS[6 + c % 2][:, t * P:(t + 1) * P], fo[:, t, c * P:(c + 1) * P], identf[:, :])
                mm.then_inc(fo_turned, 1)

            def project_out(base, n_load, src, order):
                for q in range(2):
                    loaded(pe, n_load + q)
                for k in range(8):
                    t, n = divmod(k, 2)
                    if k >= 4:
                        pe.wait_ge(x1_done, base + k - 3)
                    for j, c in enumerate(order):
                        mm = nc.tensor.matmul(PS[k % 4][:, :], src[:, c, t * P:(t + 1) * P],
                                              W[:, (n_load + n) % SLOTS, c, :], start=j == 0, stop=j == DC - 1)
                    mm.then_inc(wout_ps, 1)

            pe.wait_ge(cat_out, 4)
            pe.wait_ge(ho_step, 4)
            pe.wait_ge(co_done, 2)
            pe.wait_ge(s_done, FH * ST)
            project_out(0, 6, catT, [6, 7, 4, 5, 0, 1, 2, 3])

            pe.wait_ge(o_sb, FH * ST)
            turn(1, MT, ST)
            pe.wait_ge(turn_act, 8)
            pe.wait_ge(turn_dve, 8)
            pe.wait_ge(x1_done, 8)
            g = run([across(0, P * c, src=memT, n=M) for c in range(4)], g, 8)
            g = run([across(1, P * c, src=memT, n=M) for c in range(4)], g, 9)
            g = run([along(2, t, 0, 512, src=memT) for t in range(MT)], g, 10)
            g = run([along(3, t, 0, 512, src=memT) for t in range(MT)], g, 11)
            turn(2, ST, ST + MT)
            pe.wait_ge(turn_act, 12)
            pe.wait_ge(turn_dve, 12)
            g = run([across(0, P * c) for c in range(4)], g, 12)
            g = run([across(1, P * c) for c in range(4)], g, 13)
            pe.wait_ge(proj_out, 47)

            def x_scores(u):
                h, t = divmod(u, ST)
                if u >= 2:
                    pe.wait_ge(xe_done, u - 1)
                for k in range(2):
                    mm = nc.tensor.matmul(PS[u % 2][:, 0:M], xqT[:, 2 * h + k, t * P:(t + 1) * P], xkT[:, 2 * h + k, :],
                                          start=k == 0, stop=k == 1)
                mm.then_inc(xs_ps, 1)

            def x_turn(h):
                pe.wait_ge(xn_done, ST * (h + 1))
                for m in range(2):
                    if h:
                        pe.wait_ge(xpt_sb, 2 * (h - 1) + m + 1)
                    for t in range(ST):
                        mm = nc.tensor.transpose(PS[4 + m][:, t * P:(t + 1) * P], xp[:, t, m * P:(m + 1) * P], identf[:, :])
                    mm.then_inc(xpt_ps, 1)

            def x_pv(h):
                pe.wait_ge(xpt_sb, 2 * h + 2)
                for n in range(2):
                    gg = 2 * h + n
                    if h:
                        pe.wait_ge(xo_sb, gg - 1)
                    for m in range(2):
                        mm = nc.tensor.matmul(PS[6 + n][:, :], xv[:, m, (2 * h + n) * P:(2 * h + n + 1) * P],
                                              xpT[:, (2 * h + m) % 4, :], start=m == 0, stop=m == 1)
                    mm.then_inc(xo_ps, 1)

            for h in range(XH + 1):
                if h < XH:
                    for t in range(ST):
                        x_scores(h * ST + t)
                        if t == 1 and h:
                            pass
                    x_turn(h)
                if h >= 1:
                    x_pv(h - 1)
            pe.wait_ge(xo_sb, 8)
            project_out(8, 14, xoT, list(range(DC)))
            if STAGE == 3:
                experts_pe(pe, turn)


_INS = ["x", "mem", "mix_norm_g", "w_in", "fox_f_bias", "fox_norm_g", "hgrn_lb_logits", "hgrn_norm_g", "conv_w",
        "conv_b", "conv_norm_g", "conv_norm_b", "w_out", "xatt_norm_g", "mem_norm_g", "w_xq", "w_xkv", "w_xo",
        "ffn_norm_g", "w_group", "b_group", "w_router", "b_router", "w_gate", "w_up", "w_down", "final_norm_g"]


def kernel(**inputs):
    import numpy as _np
    import concourse.bacc as _bacc
    from concourse.bass_utils import run_bass_kernel_spmd as _run

    nc = _bacc.Bacc("TRN2", target_bir_lowering=False, num_devices=1)
    arrays, args = {}, []
    for name in _INS:
        a = _np.ascontiguousarray(inputs[name])
        arrays[f"in_{name}_dram"] = a
        args.append(nc.dram_tensor(f"in_{name}_dram", a.shape, mybir.dt.from_np(a.dtype), kind="ExternalInput").ap())
    args.append(nc.dram_tensor("out_0_dram", (1, S, D), F32, kind="ExternalOutput").ap())
    build(nc, *args)
    r = _run(nc, [arrays], core_ids=[0])
    return r.results[0]["out_0_dram"]
```

```python
from contextlib import ExitStack

import concourse.bass as bass
from concourse import mybir

F32 = mybir.dt.float32
F16 = mybir.dt.float16
BF16 = mybir.dt.bfloat16
I32 = mybir.dt.int32
U32 = mybir.dt.uint32
ALU = mybir.AluOpType
ACT = mybir.ActivationFunctionType
AX_X = mybir.AxisListType.X

P = 128
EPS = 1e-6
LOWEST = -3.0e38

D = 1024
S = 512
M = 256
FH, FD = 8, 64
FW = FH * FD
HH, HD = 4, 64
HW = HH * HD
CHUNK = 16
CC = 256
CW = 31
XH = 4
NG, NE = 4, 4
EX = NG * NE
FF = 256

DC = D // P
ST = S // P
MT = M // P
HP = HH // 2
NCH = S // CHUNK
CPT = P // CHUNK

C_FQ, C_FK, C_FV, C_FF = 0, FW, 2 * FW, 3 * FW
C_HQ = C_FF + FH
C_HF, C_HI, C_HG = C_HQ + HW, C_HQ + 2 * HW, C_HQ + 3 * HW
C_CU = C_HQ + 4 * HW
C_CG = C_CU + CC

R_MIX, R_XATT, R_MEM, R_FFN = 0, DC, 2 * DC, 3 * DC
R_FOX = 4 * DC
R_HG = R_FOX + FW // P
R_LB = R_HG + HW // P
R_CB = R_LB + HW // P
R_CNG = R_CB + CC // P
R_CNB = R_CNG + CC // P
R_CW = R_CNB + CC // P
NR = R_CW + CW * (CC // P)

SLOTS = 4
SLOT_COLS = 512
EARLY = 4


def build(nc, x, mem, mix_norm_g, w_in, fox_f_bias, fox_norm_g, hgrn_lb_logits, hgrn_norm_g,
          conv_w, conv_b, conv_norm_g, conv_norm_b, w_out, xatt_norm_g, mem_norm_g,
          w_xq, w_xkv, w_xo, ffn_norm_g, w_group, b_group, w_router, b_router,
          w_gate, w_up, w_down, final_norm_g, out):
    with ExitStack() as ctx:
        def sb(name, shape, dt=F32):
            return ctx.enter_context(nc.sbuf_tensor(name, shape, dt))

        def sem(name):
            return ctx.enter_context(nc.semaphore(name))

        x_sb = sb("x_sb", [P, ST, D])
        n_sb = sb("n_sb", [P, ST, D])
        hT = sb("hT", [P, DC, S])
        W = sb("W", [P, SLOTS, DC, SLOT_COLS])
        Dn = sb("Dn", [P, SLOTS, 2, D])
        A = sb("A", [P, 12288])
        states = sb("states", [P, NCH + 1, HD])

        identf = sb("identf", [P, P])
        identb = sb("identb", [P, P], BF16)
        causal = sb("causal", [P, P], BF16)
        chunkmask = sb("chunkmask", [P, P], I32)
        chunkcol = sb("chunkcol", [P, CPT])
        half64 = sb("half64", [P, P])
        scanmask = sb("scanmask", [P, S])
        mhalf = sb("mhalf", [P, 32])
        prow = sb("prow", [P, P])
        mixrow = sb("mixrow", [DC, P])
        pc = sb("pc", [P, NR])
        lbv = sb("lbv", [P, 4 * HP])
        wlast = sb("wlast", [P, P])
        fft = sb("fft", [P, ST, FH])
        fbias = sb("fbias", [FH, 1])
        ss = sb("ss", [P, 3 * ST + MT + ST])
        rstd = sb("rstd", [P, 3 * ST + MT + ST])
        epsb = sb("epsb", [P, 1])

        IW = HW + FH
        slot2 = W[:, 2].rearrange("p c n -> p (c n)")
        w_if = slot2[:, 0:DC * IW].rearrange("p (c n) -> p c n", c=DC)
        w_hg = slot2[:, DC * IW:DC * IW + (DC - 1) * HW].rearrange("p (c n) -> p c n", c=DC - 1)
        w_hg_last = [slot2[:, DC * IW + (DC - 1) * HW:DC * IW + (DC - 1) * HW + P], wlast[:, :]]
        qT = A[:, 0:2048].rearrange("p (c t) -> p c t", c=4)
        kT = A[:, 2048:4096].rearrange("p (c t) -> p c t", c=4)
        v = A[:, 4096:6144].rearrange("p (t n) -> p t n", t=ST)
        hqT = A[:, 6144:7168].rearrange("p (c t) -> p c t", c=HP)
        hfT = A[:, 7168:8192].rearrange("p (c t) -> p c t", c=HP)
        hgT = A[:, 8192:9216].rearrange("p (c t) -> p c t", c=HP)
        hv = A[:, 9216:10240].rearrange("p (t n) -> p t n", t=ST)
        cuT = A[:, 10240:11264].rearrange("p (c t) -> p c t", c=2)
        cgT = A[:, 11264:12288].rearrange("p (c t) -> p c t", c=2)
        fo = A[:, 6144:8192].rearrange("p (t n) -> p t n", t=ST)
        catT = n_sb[:, :, :].rearrange("p a b -> p (a b)").rearrange("p (c t) -> p c t", c=DC)
        scr = Dn[:, :, :, :].rearrange("p a b c -> p (a b c)").rearrange("p (n c t) -> p n c t", n=8, c=HP)
        hk, hgl, hb, hd1, he1, he2, he3, he4 = (scr[:, n] for n in range(8))
        khtok = hd1.rearrange("p c (t k) -> p c t k", t=ST)
        attm = Dn[:, 0:2].rearrange("p a b c -> p (a b c)")[:, 1024:3072].rearrange("p (h t s) -> p h t s", h=HH, t=ST)
        vexp = [hk.rearrange("p a (b n) -> p (a b n)", n=HD).rearrange("p (h n v) -> p h n v", h=2, n=CPT),
                hfT.rearrange("p a (b n) -> p (a b n)", n=HD).rearrange("p (h n v) -> p h n v", h=2, n=CPT)]
        hTf = hT[:, :, :].rearrange("p c t -> p (c t)")
        fs = [hTf[:, 0:512], hTf[:, 512:1024], hTf[:, 3328:3840]]
        fpT = [hTf[:, 1024:1536], hTf[:, 1536:2048]]
        fnegc = [hTf[:, 2048:2560], hTf[:, 2560:3072]]
        fsq = hTf[:, 3072:3328].rearrange("p (t v) -> p t v", t=ST)
        lfa, lfb, ones8 = (catT[0:FH, c] for c in range(3))
        fmx = sb("fmx", [P, 32])
        fnm = sb("fnm", [P, 32])
        frs = sb("frs", [P, 32])
        frr = sb("frr", [P, 32])
        fss = sb("fss", [P, 32])
        frstd = sb("frstd", [P, 32])
        xqT = A[:, 0:4096].rearrange("p (c t) -> p c t", c=DC)
        xv = A[:, 8192:10240].rearrange("p (t n) -> p t n", t=MT)
        xkT = A[:, 10240:12288].rearrange("p (c m) -> p c m", c=DC)
        mem_sb = Dn[:, 0]
        memT = Dn[:, 1].rearrange("p a b -> p (a b)").rearrange("p (c m) -> p c m", c=DC)
        xoT = catT
        xp = Dn[:, 2].rearrange("p a b -> p (a b)").rearrange("p (h n m) -> p h n m", h=2, n=ST)
        xpT = Dn[:, 0].rearrange("p a b -> p (a b)").rearrange("p (c t) -> p c t", c=4)
        nA = A[:, 0:4096].rearrange("p (t d) -> p t d", t=ST)
        junk = A[:, 5632:7680].rearrange("p (b d) -> p b d", b=2)
        xg = A[:, 0:2048].rearrange("p (b d) -> p b d", b=2)
        xgT = A[:, 2048:4096].rearrange("p (b c t) -> p b c t", b=2, c=DC)
        sg = A[:, 4096:4608].rearrange("p (b f) -> p b f", b=2)
        hid = A[:, 4608:5120].rearrange("p (b f) -> p b f", b=2)
        hidT = A[:, 5120:5632].rearrange("p (b k t) -> p b k t", b=2, k=2)
        ysb = A[:, 5632:7680].rearrange("p (b d) -> p b d", b=2)
        fgain = A[:, 7680:8704]
        room = [8704]

        def small(*shape, dt=F32, parts=P):
            n = 1
            for k in shape:
                n *= k
            at = room[0]
            room[0] += n
            ap = A[0:parts, at:at + n]
            if dt is not F32:
                ap = ap.bitcast(dt)
            names = " ".join("abc"[:len(shape)])
            return ap.rearrange(f"p ({names}) -> p {names}", **{k: m for k, m in zip("abc", shape)}) if len(shape) > 1 else ap

        logits = small(ST, NG + EX)
        beats, ties = small(ST, 4, 4), small(ST, 4, 4)
        grank, ghot, erank, ehot = small(ST, 4), small(ST, 4), small(ST, 4), small(ST, 4)
        gtop, gsum, etop, esum = small(ST), small(ST), small(ST), small(ST)
        gexp, esel, eexp = small(ST, 4), small(ST, 4), small(ST, 4)
        spread = small(ST, 4, 4)
        picked, weight = small(ST, EX), small(ST, EX)
        pos, posm, slot, part = small(ST, EX), small(ST, EX), small(ST, EX), small(ST, EX)
        stop_, ssum_, w1st, w2nd = small(ST), small(ST), small(ST), small(ST)
        token_of = small(EX, dt=U32)
        slot1, slot2 = small(ST, dt=U32), small(ST, dt=U32)
        most = small(1)
        over = small(1, dt=I32)
        ov_token = small(1, dt=U32)
        pickedb = A[:, room[0]:room[0] + 32].bitcast(BF16).rearrange("p (t e) -> p t e", t=ST)
        posm16 = A[:, room[0] + 32:room[0] + 64].bitcast(F16).rearrange("p (t e) -> p t e", t=ST)
        lgT = A[0:NG + EX, 10240:10240 + S]
        srow = states[:, 17:, :].rearrange("p a b -> p (a b)")
        wgr = srow[:, 0:160].rearrange("p (c n) -> p c n", c=DC)
        rbias = srow[:, 160:180]
        ranks = srow[:, 192:320]
        before = srow[:, 320:384].bitcast(BF16)
        onesb = srow[:, 384:448].bitcast(BF16)
        lower = srow[:, 448:464].rearrange("p (i j) -> p i j", i=4)
        ebase = srow[:, 464:480]
        tokid = srow[:, 480:482].bitcast(F16)
        ranks16 = srow[:, 484:548].bitcast(F16)
        pick = hTf.bitcast(F16).rearrange("p (t e r) -> p t e r", t=ST, e=EX)
        ov_pick = hTf.bitcast(F16)[:, 0:ST * P].rearrange("p (t r) -> p t r", t=ST)
        ygath = W[:, 0:2].rearrange("p a b c -> p (a b c)").rearrange("p (t k d) -> p t k d", t=ST, k=2)

        n_dram = nc.dram_tensor("n_dram", (S, D), F32, kind="Internal").ap()
        y_dram = nc.dram_tensor("y_dram", (ST * EX * P, D), F32, kind="Internal").ap()
        y_rows = y_dram.rearrange("(e p) d -> e p d", p=P)

        PS = [ctx.enter_context(nc.psum_tensor(f"bank{i}", [P, 512], F32)) for i in range(8)]

        x_in = [sem(f"x_in{t}") for t in range(ST)]
        mix_in = sem("mix_in")
        params_in = sem("params_in")
        mem_in = sem("mem_in")
        w_in_slot = [sem(f"w_loaded{i}") for i in range(SLOTS)]
        const_step = sem("const_step")
        consts = sem("consts")
        pcol = sem("pcol")
        pcol_ps = sem("pcol_ps")
        lb_step = sem("lb_step")
        sq_done = sem("sq_done")
        ms_done = sem("ms_done")
        rstd_done = sem("rstd_done")
        n_done = sem("n_done")
        turned = sem("turned")
        turn_sb = sem("turn_sb")
        hi_in = sem("hi_in")
        ff_sb = sem("ff_sb")
        proj = sem("proj")
        proj_out = sem("proj_out")
        conv_a = sem("conv_a")
        conv_y = sem("conv_y")
        cmean = sem("cmean")
        cdev = sem("cdev")
        cvar = sem("cvar")
        crs = sem("crs")
        cz = sem("cz")
        co_done = sem("co_done")
        hf_done = sem("hf_done")
        hg_log = sem("hg_log")
        hb_done = sem("hb_done")
        hd_done = sem("hd_done")
        he_done = sem("he_done")
        hprod = sem("hprod")
        kh_turned = sem("kh_turned")
        kh_out = sem("kh_out")
        vexp_done = sem("vexp_done")
        u_done = sem("u_done")
        state_step = sem("state_step")
        att_ps = sem("att_ps")
        att_zero = sem("att_zero")
        att_done = sem("att_done")
        ho_ps = sem("ho_ps")
        ho_sb = sem("ho_sb")
        ho_sq = sem("ho_sq")
        ho_ms = sem("ho_ms")
        ho_rs = sem("ho_rs")
        ho_step = sem("ho_step")
        lf_act = sem("lf_act")
        lf_dve = sem("lf_dve")
        negc_ps = sem("negc_ps")
        negc_sb = sem("negc_sb")
        qk_done = sem("qk_done")
        s_done = sem("s_done")
        m_done = sem("m_done")
        p_done = sem("p_done")
        pt_ps = sem("pt_ps")
        pt_act = sem("pt_act")
        pt_dve = sem("pt_dve")
        o_ps = sem("o_ps")
        o_sb = sem("o_sb")
        f_step = sem("f_step")
        f_ms = sem("f_ms")
        f_rstd = sem("f_rstd")
        fo_turned = sem("fo_turned")
        cat_out = sem("cat_out")
        wout_ps = sem("wout_ps")
        x1_done = sem("x1_done")
        xs_ps = sem("xs_ps")
        xm_done = sem("xm_done")
        xe_done = sem("xe_done")
        xr_done = sem("xr_done")
        xn_done = sem("xn_done")
        xpt_ps = sem("xpt_ps")
        xpt_sb = sem("xpt_sb")
        xo_ps = sem("xo_ps")
        xo_sb = sem("xo_sb")
        out_done = sem("out_done")
        f_normed = sem("f_normed")
        router_in = sem("router_in")
        router_const = sem("router_const")
        router_step = sem("router_step")
        lgt_ps = sem("lgt_ps")
        lgt_sb = sem("lgt_sb")
        logits_ps = sem("logits_ps")
        route = sem("route")
        soft_in = sem("soft_in")
        soft_out = sem("soft_out")
        picked_done = sem("picked_done")
        pos_ps = sem("pos_ps")
        pick_done = sem("pick_done")
        token_ps = sem("token_ps")
        token_done = sem("token_done")
        over_done = sem("over_done")
        slots_done = sem("slots_done")
        n_stored = sem("n_stored")
        dn_loaded = [sem(f"dn_loaded{i}") for i in range(SLOTS)]
        xg_in = [sem(f"xg_in{i}") for i in range(2)]
        xt_ps = sem("xt_ps")
        xt_sb = sem("xt_sb")
        gu_ps = sem("gu_ps")
        silu_done = sem("silu_done")
        hid_done = sem("hid_done")
        ht_ps = sem("ht_ps")
        ht_sb = sem("ht_sb")
        y_ps = sem("y_ps")
        y_act = sem("y_act")
        y_dve = sem("y_dve")
        y_stored = [sem(f"y_stored{i}") for i in range(2)]
        ov_pos = sem("ov_pos")
        ov_picked = sem("ov_picked")
        ov_token_ps = sem("ov_token_ps")
        ov_token_sb = sem("ov_token_sb")
        ov_xg = sem("ov_xg")
        ov_w = sem("ov_w")
        ov_xt_ps = sem("ov_xt_ps")
        ov_xt_sb = sem("ov_xt_sb")
        ov_gu = sem("ov_gu")
        ov_silu = sem("ov_silu")
        ov_hid = sem("ov_hid")
        ov_ht_ps = sem("ov_ht_ps")
        ov_ht_sb = sem("ov_ht_sb")
        ov_y_ps = sem("ov_y_ps")
        ov_y_sb = sem("ov_y_sb")
        ov_stored = sem("ov_stored")
        fin_in = [[sem(f"fin{k}_in{t}") for k in range(2)] for t in range(ST)]
        fin_sum = sem("fin_sum")
        fin_sq = sem("fin_sq")
        fin_ms = sem("fin_ms")
        fin_root = sem("fin_root")
        fin_out = sem("fin_out")
        half_done = sem("half_done")
        ones_done = sem("ones_done")
        xs_step = sem("xs_step")
        f_sq_step = sem("f_sq_step")
        root_step = sem("root_step")
        croot = [cgT[:, 0], cgT[:, 1]]
        KV_AT = [1, 3, 5, 7, 10, 14, 17, 19, 23, 27, 31]
        FO_AT = {24: 1, 28: 0, 32: 2}
        LAG = 2
        hob = [he4[:, 0], he4[:, 1]]
        hrb = [he2[:, 0], he2[:, 1]]

        def rows(w):
            return w.rearrange("(c p) n -> p c n", p=P)

        win, wout, wxq, wxkv, wxo = rows(w_in[0]), rows(w_out[0]), rows(w_xq[0]), rows(w_xkv[0]), rows(w_xo[0])
        LOADS = [(win, C_CU), (win, C_HQ), (win, C_HI), (win, C_FQ), (win, C_FK), (win, C_FV),
                 (wxkv, 0), (wxkv, 512), (wxkv, 1024), (wxkv, 1536), (wout, 0), (wout, 512),
                 (wxq, 0), (wxq, 512), (wxo, 0), (wxo, 512)]

        def loaded(eng, n):
            eng.wait_ge(w_in_slot[n % SLOTS], 16 * (n // SLOTS + 1))

        GROUPS = {0: 4, 1: 8, 2: 15, 3: 19, 4: 23, 5: 27, 6: 31, 7: 35, 8: 37, 9: 39, 12: 43, 13: 47}

        def freed(n):
            return (proj, GROUPS[n]) if n in GROUPS else (wout_ps, 8 if n < 12 else 16)

        NORM0 = [0, ST, ST + MT, 2 * ST + MT]
        TURN0 = [2 * n for n in NORM0]
        XKV0, XQ0, GROUPS_END = 27, 39, 47

        def bank_of(g):
            return g % 4 if g < 16 else 7 if XKV0 <= g < XQ0 - 1 else g % 2

        def bank_free(pe, g):
            former = [k for k in range(g) if bank_of(k) == bank_of(g)]
            if former:
                pe.wait_ge(proj_out, former[-1] + 1)

        wg_e = w_gate.rearrange("l g e (c p) f -> (l g e) p c f", p=P)
        wu_e = w_up.rearrange("l g e (c p) f -> (l g e) p c f", p=P)
        wd_e = w_down.rearrange("l g e (k p) d -> (l g e) p k d", p=P)

        def load_gate_up(sp, e, s, done):
            sp.dma_start(W[:, s, :, 0:FF], wg_e[e]).then_inc(done, 16)
            sp.dma_start(W[:, s, :, FF:2 * FF], wu_e[e]).then_inc(done, 16)

        def gate_up_loaded(eng, s, turn_):
            eng.wait_ge(w_in_slot[s], 16 * len(LOADS) // SLOTS + 32 + 32 * turn_)

        block = ctx.enter_context(nc.Block())

        def parameters(sp):
            pr = [(mix_norm_g, R_MIX), (xatt_norm_g, R_XATT), (None, R_MEM), (ffn_norm_g, R_FFN), (fox_norm_g, R_FOX),
                  (hgrn_norm_g, R_HG), (hgrn_lb_logits, R_LB), (conv_b, R_CB), (conv_norm_g, R_CNG), (conv_norm_b, R_CNB)]
            for src, r in pr:
                row = mem_norm_g if src is None else src[0]
                k = row.shape[0] // P
                sp.dma_start(prow[r:r + k, :], row.rearrange("(c p) -> c p", p=P)).then_inc(params_in, 16)
            sp.dma_start(prow[R_CW:NR, :], conv_w[0].rearrange("w (c p) -> (w c) p", p=P)).then_inc(params_in, 16)
            sp.dma_start(fbias[:, :], fox_f_bias[0].rearrange("(h o) -> h o", o=1)).then_inc(params_in, 16)

        def experts_loads(sp):
            sp.wait_ge(x1_done, 8)
            for e in (1, 3):
                sp.dma_start(Dn[:, e], wd_e[e]).then_inc(dn_loaded[e], 16)
            for e in range(2):
                sp.wait_ge(*freed(12 + e))
                load_gate_up(sp, e, e, w_in_slot[e])
            sp.wait_ge(xo_ps, 2 * XH)
            for e in (0, 2):
                sp.dma_start(Dn[:, e], wd_e[e]).then_inc(dn_loaded[e], 16)
            for t in range(ST):
                sp.wait_ge(n_done, NORM0[3] + t + 1)
                sp.dma_start(n_dram[t * P:(t + 1) * P, :], nA[:, t, :]).then_inc(n_stored, 16)
            sp.dma_start(fgain, final_norm_g.rearrange("(o d) -> o d", o=1).to_broadcast([P, D])).then_inc(router_in, 16)
            for e in range(2, SLOTS):
                sp.wait_ge(*freed(12 + e))
                load_gate_up(sp, e, e, w_in_slot[e])

            def step(e, s, nxt):
                if nxt:
                    sp.wait_ge(gu_ps, e + 1)
                    load_gate_up(sp, e + SLOTS, s, w_in_slot[s])
                    sp.wait_ge(y_ps, 2 * e + 2)
                    sp.dma_start(Dn[:, s], wd_e[e + SLOTS]).then_inc(dn_loaded[s], 16)
                sp.wait_ge(y_act, e + 1)
                sp.wait_ge(y_dve, e + 1)
                sp.dma_start(y_rows[e], ysb[:, s % 2]).then_inc(y_stored[s % 2], 16)

            with sp.Fori(0, EX // SLOTS - 1) as i:
                for j in range(SLOTS):
                    step(i * SLOTS + j, j, True)
            for j in range(SLOTS):
                step(EX - SLOTS + j, j, False)

            sp.wait_ge(over_done, 1)
            with sp.If(sp.value_load(over[0:1, 0:1]) > 0):
                sp.wait_ge(y_ps, 2 * EX)
                with sp.Fori(0, (ST - 1) * EX) as k:
                    e = k % EX
                    sp.dma_start(W[:, 0, :, 0:FF], wg_e[e]).then_inc(ov_w, 16)
                    sp.dma_start(W[:, 0, :, FF:2 * FF], wu_e[e]).then_inc(ov_w, 16)
                    sp.dma_start(Dn[:, 0], wd_e[e]).then_inc(ov_w, 16)
                    sp.wait_ge(ov_y_sb, 2 * k + 2)
                    sp.dma_start(y_rows[k + EX], ysb[:, 0]).then_inc(ov_stored, 16)
            with sp.Else():
                pass
            for t in range(ST):
                sp.wait_ge(fin_out, t + 1)
                sp.dma_start(out[0, t * P:(t + 1) * P, :], n_sb[:, t, :]).then_inc(out_done, 16)
            sp.wait_ge(out_done, 16 * ST)

        @block.sync
        def _(sp):
            for t in range(ST):
                sp.dma_start(x_sb[:, t, :], x[0, t * P:(t + 1) * P, :]).then_inc(x_in[t], 16)
                if t == 0:
                    sp.dma_start(mixrow[:, :], mix_norm_g[0].rearrange("(c p) -> c p", p=P)).then_inc(mix_in, 16)
            parameters(sp)
            for n, (src, c0) in enumerate(LOADS):
                if n >= SLOTS:
                    sp.wait_ge(*freed(n - SLOTS))
                if c0 == C_HI and src is win:
                    sp.dma_start(w_if[:, :, 0:HW], win[:, :, C_HI:C_HI + HW]).then_inc(w_in_slot[2], 16)
                    sp.dma_start(w_if[:, :, HW:IW], win[:, :, C_FF:C_FF + FH]).then_inc(hi_in, 16)
                    sp.dma_start(w_hg, win[:, 0:DC - 1, C_HG:C_HG + HW]).then_inc(hi_in, 16)
                    for k in range(2):
                        sp.dma_start(w_hg_last[k], win[:, DC - 1, C_HG + k * P:C_HG + (k + 1) * P]).then_inc(hi_in, 16)
                else:
                    sp.dma_start(W[:, n % SLOTS], src[:, :, c0:c0 + SLOT_COLS]).then_inc(w_in_slot[n % SLOTS], 16)
                if n == 8:
                    sp.wait_ge(ho_ps, 2)
                    sp.dma_start(mem_sb, mem[0].rearrange("(t p) d -> p t d", p=P)).then_inc(mem_in, 16)
                if n == 9:
                    sp.dma_start(wgr[:, :, 0:NG], rows(w_group[0])).then_inc(router_in, 16)
                    sp.dma_start(wgr[:, :, NG:], rows(w_router[0])).then_inc(router_in, 16)
                    sp.dma_start(rbias[:, 0:NG], b_group.to_broadcast([P, NG])).then_inc(router_in, 16)
                    sp.dma_start(rbias[:, NG:], b_router.to_broadcast([P, EX])).then_inc(router_in, 16)
            experts_loads(sp)

        def experts_gathers(pool):
            root(pool, 3, ST)
            pool.wait_ge(n_stored, 16 * ST)
            pool.wait_ge(token_done, 1)
            for e in range(EX):
                if e == EARLY:
                    pool.wait_ge(token_done, 2)
                if e >= 2:
                    pool.wait_ge(xt_ps, 2 * (e - 1))
                nc.gpsimd.indirect_dma_start(out=xg[:, e % 2, :], out_offset=None, in_=n_dram,
                                             in_offset=bass.IndirectOffsetOnAxis(ap=token_of[:, e:e + 1], axis=0)).then_inc(xg_in[e % 2], 16)
            def final_root(t):
                pool.wait_ge(fin_ms, t + 1)
                f = 3 * ST + MT + t
                nc.gpsimd.tensor_tensor(rstd[:, f:f + 1], ss[:, f:f + 1], mhalf[:, 0:1], ALU.pow).then_inc(fin_root, 1)

            def gather_rows(k, sl, written):
                for t in range(ST):
                    nc.gpsimd.indirect_dma_start(out=ygath[:, t, k, :], out_offset=None, in_=written,
                                                 in_offset=bass.IndirectOffsetOnAxis(ap=sl[:, t:t + 1], axis=0)).then_inc(fin_in[t][k], 16)

            pool.wait_ge(over_done, 1)
            with pool.If(pool.value_load(over[0:1, 0:1]) > 0):
                pool.wait_ge(xt_ps, 2 * EX)
                for k in range((ST - 1) * EX):
                    pool.wait_ge(ov_token_sb, k + 1)
                    nc.gpsimd.indirect_dma_start(out=xg[:, 0, :], out_offset=None, in_=n_dram,
                                                 in_offset=bass.IndirectOffsetOnAxis(ap=ov_token[:, 0:1], axis=0)).then_inc(ov_xg, 16)
                pool.wait_ge(ov_stored, 16 * (ST - 1) * EX)
                pool.wait_ge(y_stored[0], 16 * EX // 2)
                pool.wait_ge(y_stored[1], 16 * EX // 2)
                pool.wait_ge(slots_done, 2)
                gather_rows(0, slot1, y_dram)
                gather_rows(1, slot2, y_dram)
            with pool.Else():
                pool.wait_ge(y_stored[0], 16 * EX // 2)
                pool.wait_ge(y_stored[1], 16 * (EX // 2 - 1))
                pool.wait_ge(slots_done, 2)
                pool.wait_ge(gu_ps, EX - 2)
                gather_rows(0, slot1, y_dram[0:(EX - 1) * P, :])
                pool.wait_ge(y_stored[1], 16 * EX // 2)
                gather_rows(1, slot2, y_dram[0:EX * P, :])
            for t in range(ST):
                final_root(t)

        def root(pool, stage, tiles):
            for n in range(NORM0[stage], NORM0[stage] + tiles):
                pool.wait_ge(ms_done, n + 1)
                nc.gpsimd.tensor_tensor(rstd[:, n:n + 1], ss[:, n:n + 1], mhalf[:, 0:1], ALU.pow).then_inc(rstd_done, 1)

        @block.gpsimd
        def _(pool):
            nc.gpsimd.memset(identf[:, :], 0.0).then_inc(const_step, 1)
            nc.gpsimd.memset(identb[:, :], 0.0).then_inc(const_step, 1)
            nc.gpsimd.memset(causal[:, :], 0.0).then_inc(const_step, 1)
            nc.gpsimd.memset(chunkmask[:, :], 1).then_inc(const_step, 1)
            nc.gpsimd.memset(chunkcol[:, :], 1.0).then_inc(const_step, 1)
            nc.gpsimd.memset(scanmask[:, :], 1.0).then_inc(const_step, 1)
            nc.gpsimd.memset(mhalf[:, :], -0.5).then_inc(consts, 1)
            nc.gpsimd.memset(epsb[:, :], EPS).then_inc(consts, 1)
            pool.wait_ge(const_step, 6)
            for m in (identf, identb):
                nc.gpsimd.affine_select(out=m[:, :], in_=m[:, :], compare_op=ALU.not_equal, fill=1.0, base=0,
                                        pattern=[[-1, P]], channel_multiplier=1).then_inc(consts, 1)
            nc.gpsimd.affine_select(out=causal[:, :], in_=causal[:, :], compare_op=ALU.is_ge, fill=-1e30, base=0,
                                    pattern=[[-1, P]], channel_multiplier=1).then_inc(consts, 1)
            nc.gpsimd.affine_select(out=chunkmask[:, :], in_=chunkmask[:, :], compare_op=ALU.is_ge, fill=0, base=0,
                                    pattern=[[1, P]], channel_multiplier=-1).then_inc(const_step, 1)
            nc.gpsimd.affine_select(out=chunkcol[:, :], in_=chunkcol[:, :], compare_op=ALU.is_ge, fill=0.0, base=0,
                                    pattern=[[-CHUNK, CPT]], channel_multiplier=1).then_inc(const_step, 1)
            nc.gpsimd.memset(scanmask[:, :].rearrange("p (n j) -> p n j", j=CHUNK)[:, :, 0:1], 0.0).then_inc(consts, 1)
            pool.wait_ge(const_step, 8)
            nc.gpsimd.affine_select(out=chunkmask[:, :], in_=chunkmask[:, :], compare_op=ALU.is_ge, fill=0, base=0,
                                    pattern=[[-CHUNK, CPT], [0, CHUNK]], channel_multiplier=1).then_inc(consts, 1)
            nc.gpsimd.affine_select(out=chunkcol[:, :], in_=chunkcol[:, :], compare_op=ALU.is_ge, fill=0.0,
                                    base=CHUNK - 1, pattern=[[CHUNK, CPT]], channel_multiplier=-1).then_inc(consts, 1)

            root(pool, 0, ST)

            for p in range(HP):
                pool.wait_ge(he_done, 4 * p + 4)
                pool.wait_ge(hf_done, 2 * p + 2)
                pool.wait_ge(proj_out, 8)
                nc.gpsimd.tensor_tensor(he3[:, p], he3[:, p], hk[:, p], ALU.mult).then_inc(hprod, 1)
                nc.gpsimd.tensor_tensor(he2[:, p], he2[:, p], hk[:, p], ALU.mult).then_inc(hprod, 1)
                nc.gpsimd.tensor_tensor(he1[:, p], he1[:, p], hqT[:, p], ALU.mult).then_inc(hprod, 1)
                pool.wait_ge(hprod, 4 * p + 3)
                nc.gpsimd.tensor_tensor(hqT[:, p], hqT[:, p], he4[:, p], ALU.mult).then_inc(hprod, 1)
            pool.wait_ge(hprod, 4 * HP)
            pool.wait_ge(proj_out, 12)
            for p in range(HP):
                for t in range(ST):
                    i = p * ST + t
                    if i >= 2:
                        pool.wait_ge(u_done, i - 1)
                    for a in range(2):
                        h = 2 * p + a
                        vsrc = hv[:, t, h * HD:(h + 1) * HD].rearrange("p (o v) -> p o v", o=1).to_broadcast([P, CPT, HD])
                        csrc = chunkcol[:, :].rearrange("p (n o) -> p n o", o=1).to_broadcast([P, CPT, HD])
                        nc.gpsimd.tensor_tensor(vexp[i % 2][:, a], vsrc, csrc, ALU.mult).then_inc(vexp_done, 1)

            root(pool, 1, MT)
            for h in range(FH):
                pool.wait_ge(f_ms, h + 1)
                nc.gpsimd.tensor_tensor(frstd[:, 4 * h:4 * h + 4], fss[:, 4 * h:4 * h + 4], mhalf[:, 0:4],
                                        ALU.pow).then_inc(f_rstd, 1)
            pool.wait_ge(ho_ps, 2)
            nc.gpsimd.iota(ranks, pattern=[[1, P]], base=0, channel_multiplier=0,
                               allow_small_or_imprecise_dtypes=True).then_inc(router_const, 1)
            nc.gpsimd.iota(ranks16, pattern=[[1, P]], base=0, channel_multiplier=0,
                               allow_small_or_imprecise_dtypes=True).then_inc(router_const, 1)
            nc.gpsimd.iota(tokid, pattern=[[P, ST]], base=0, channel_multiplier=1,
                               allow_small_or_imprecise_dtypes=True).then_inc(router_const, 1)
            nc.gpsimd.iota(ebase, pattern=[[P, EX]], base=0, channel_multiplier=0,
                               allow_small_or_imprecise_dtypes=True).then_inc(router_const, 1)
            nc.gpsimd.memset(before, 1.0).then_inc(router_step, 1)
            nc.gpsimd.memset(lower, 1.0).then_inc(router_step, 1)
            nc.gpsimd.memset(onesb, 1.0).then_inc(router_const, 1)
            pool.wait_ge(router_step, 2)
            nc.gpsimd.affine_select(out=before, in_=before, compare_op=ALU.is_gt, fill=0.0, base=0,
                                    pattern=[[1, P]], channel_multiplier=-1).then_inc(router_const, 1)
            nc.gpsimd.affine_select(out=lower, in_=lower, compare_op=ALU.is_gt, fill=0.0, base=0,
                                    pattern=[[1, 4], [-1, 4]], channel_multiplier=0).then_inc(router_const, 1)
            root(pool, 2, ST)
            experts_gathers(pool)

        def square(act, stage, t, src, dst):
            n = NORM0[stage] + t
            nc.scalar.activation(dst, src[:, t, :], ACT.Square, accum_out=ss[:, n:n + 1]).then_inc(sq_done, 1)

        def experts_act(act):
            for t in range(ST):
                act.wait_ge(x1_done, 8 + 2 * t + 2)
                square(act, 3, t, x_sb, junk[:, t % 2])
                for u in ([], [], [0], [1, 2, 3])[t]:
                    act.wait_ge(lgt_ps, u + 1)
                    nc.scalar.activation(lgT[:, u * P:(u + 1) * P], PS[4 + 2 * u % 4][0:NG + EX, 0:P], ACT.Copy).then_inc(lgt_sb, 1)
            act.wait_ge(soft_in, 1)
            nc.scalar.activation(gexp, gexp, ACT.Exp).then_inc(soft_out, 1)
            act.wait_ge(soft_in, 2)
            nc.scalar.activation(eexp, eexp, ACT.Exp).then_inc(soft_out, 1)

            def silu(e, b, first):
                act.wait_ge(gu_ps, e + 1)
                if not first:
                    act.wait_ge(hid_done, e - 1)
                nc.scalar.activation(sg[:, b], PS[2 + b][:, 0:FF], ACT.Silu).then_inc(silu_done, 1)

            def turned_hid(e, b, first):
                act.wait_ge(ht_ps, e + 1)
                if not first:
                    act.wait_ge(y_ps, 2 * (e - 1))
                nc.scalar.activation(hidT[:, b], PS[4][:, 0:2 * P].rearrange("p (k t) -> p k t", k=2), ACT.Copy).then_inc(ht_sb, 1)

            def y_half(e, b, first):
                act.wait_ge(y_ps, 2 * e + 1)
                if not first:
                    act.wait_ge(y_stored[b], 16 * ((e + (-b)) // 2))
                nc.scalar.activation(ysb[:, b, 0:512], PS[5][:, :], ACT.Copy).then_inc(y_act, 1)

            def step(e, j, start):
                silu(e, j % 2, start and j < 2)
                if not (start and j == 0):
                    y_half(e - 1, (j + 1) % 2, start and j < 3)
                turned_hid(e, j % 2, start and j < 2)

            for j in range(SLOTS):
                step(j, j, True)
            with act.Fori(1, EX // SLOTS) as i:
                for j in range(SLOTS):
                    step(i * SLOTS + j, j, False)
            y_half(EX - 1, 1, False)

            act.wait_ge(over_done, 1)
            with act.If(act.value_load(over[0:1, 0:1]) > 0):
                act.wait_ge(y_stored[0], 16 * EX // 2)
                act.wait_ge(y_stored[1], 16 * EX // 2)
                with act.Fori(0, (ST - 1) * EX) as k:
                    act.wait_ge(ov_gu, k + 1)
                    nc.scalar.activation(sg[:, 0], PS[2][:, 0:FF], ACT.Silu).then_inc(ov_silu, 1)
                    act.wait_ge(ov_ht_ps, k + 1)
                    nc.scalar.activation(hidT[:, 0], PS[4][:, 0:2 * P].rearrange("p (k t) -> p k t", k=2), ACT.Copy).then_inc(ov_ht_sb, 1)
                    act.wait_ge(ov_y_ps, 2 * k + 2)
                    nc.scalar.activation(ysb[:, 0, 0:512], PS[5][:, :], ACT.Copy).then_inc(ov_y_sb, 1)
                    nc.scalar.activation(ysb[:, 0, 512:1024], PS[6][:, :], ACT.Copy).then_inc(ov_y_sb, 1)
                    act.wait_ge(ov_stored, 16 * k + 16)
            with act.Else():
                pass
            for t in range(ST):
                act.wait_ge(fin_sum, ST + t + 1)
                nc.scalar.activation(n_sb[:, t, :], x_sb[:, t, :], ACT.Square, 
                                     accum_out=ss[:, NORM0[3] + ST + t:NORM0[3] + ST + t + 1]).then_inc(fin_sq, 1)

        PROJ = ([("t", cuT[:, c], ACT.Copy) for c in range(2)] + [("t", cgT[:, c], ACT.Sigmoid) for c in range(2)]
                + [("t", hqT[:, c], ACT.Copy) for c in range(2)] + [("t", hfT[:, c], ACT.Sigmoid) for c in range(2)]
                + [("hv", hv[:, t], ACT.Copy) for t in range(ST)] + [("ff", lfa[:, :], ACT.Copy)] + [("t", hgT[:, c], ACT.Silu) for c in range(2)]
                + [("q", qT[:, c], ACT.Copy) for c in range(4)] + [("t", kT[:, c], ACT.Copy) for c in range(4)]
                + [("n", v[:, t], ACT.Copy) for t in range(ST)])

        @block.scalar
        def _(act):
            for t in range(ST):
                act.wait_ge(x_in[t], 16)
                square(act, 0, t, x_sb, n_sb[:, t, :])

            def proj_evac(g0, g1):
                for g in range(g0, g1):
                    kind, dst, fn = PROJ[g]
                    act.wait_ge(proj, g + 1)
                    if kind == "hv":
                        nc.scalar.activation(fft[:, g - 8, :], PS[bank_of(g)][:, HW:IW], ACT.Copy).then_inc(ff_sb, 1)
                    if kind == "ff":
                        nc.scalar.activation(dst, PS[bank_of(g)][0:FH, :], ACT.Copy).then_inc(proj_out, 1)
                    elif kind == "q":
                        nc.scalar.activation(dst, PS[bank_of(g)][:, :], fn, scale=FD ** -0.5).then_inc(proj_out, 1)
                    else:
                        w = dst.shape[-1]
                        nc.scalar.activation(dst, PS[bank_of(g)][:, 0:w], fn).then_inc(proj_out, 1)

            proj_evac(0, 8)
            for p in range(HP):
                act.wait_ge(hf_done, 2 * p + 1)
                nc.scalar.activation(hgl[:, p], hfT[:, p], ACT.Ln).then_inc(hg_log, 1)
            proj_evac(8, 13)
            for p in range(HP):
                act.wait_ge(hd_done, 2 * p + 1)
                nc.scalar.activation(he1[:, p], hd1[:, p], ACT.Exp).then_inc(he_done, 1)
                nc.scalar.activation(he2[:, p], hd1[:, p], ACT.Exp, scale=-1.0).then_inc(he_done, 1)
                act.wait_ge(hd_done, 2 * p + 2)
                nc.scalar.activation(he3[:, p], hgl[:, p], ACT.Exp, scale=-1.0).then_inc(he_done, 1)
                nc.scalar.activation(he4[:, p], hb[:, p], ACT.Exp).then_inc(he_done, 1)
            act.wait_ge(lf_dve, 3)
            nc.scalar.activation(lfb[:, :], lfb[:, :], ACT.Exp, scale=-1.0).then_inc(lf_act, 1)
            act.wait_ge(lf_act, 1)
            nc.scalar.activation(lfb[:, :], lfb[:, :], ACT.Ln, bias=1.0).then_inc(lf_act, 1)
            proj_evac(13, 17)
            for p in range(HP):
                act.wait_ge(kh_turned, p + 1)
                nc.scalar.activation(khtok[:, p], PS[4 + p][:, :].rearrange("p (t k) -> p t k", t=ST), ACT.Copy).then_inc(kh_out, 1)

            def ho_evac(p):
                act.wait_ge(ho_ps, p + 1)
                act.wait_ge(state_step, 1 + CPT * ST * (p + 1))
                nc.scalar.activation(hob[p], PS[6 + p][:, :], ACT.Copy).then_inc(ho_sb, 1)

            def inv_root(k, src, dst, done):
                nc.scalar.activation(dst, src, ACT.Ln, bias=epsb[:, 0:1]).then_inc(root_step, 1)
                act.wait_ge(root_step, k + 1)
                nc.scalar.activation(dst, dst, ACT.Exp, scale=-0.5).then_inc(done, 1)

            proj_evac(17, 21)
            ho_evac(0)
            proj_evac(21, 22)
            act.wait_ge(consts, 2)
            for c in range(2):
                act.wait_ge(cvar, c + 1)
                inv_root(c, PS[4 + c][:, :], croot[c], crs)
            proj_evac(22, 24)
            ho_evac(1)
            proj_evac(24, 25)
            act.wait_ge(mem_in, 16)
            for t in range(MT):
                square(act, 1, t, mem_sb, Dn[:, 1, t, :])
            for p in range(HP):
                act.wait_ge(ho_ms, p + 1)
                inv_root(2 + p, PS[4 + p][:, :], hrb[p], ho_rs)
            proj_evac(25, 26)
            for c in range(2):
                act.wait_ge(cz, c + 1)
                nc.scalar.activation(catT[:, 6 + c], cuT[:, c], ACT.Silu, bias=pc[:, R_CNB + c:R_CNB + c + 1],
                                     scale=pc[:, R_CNG + c:R_CNG + c + 1]).then_inc(co_done, 1)
            proj_evac(26, 27)
            def f_exp(u):
                h, i = divmod(u, ST)
                act.wait_ge(m_done, u + 1)
                w = P * (i + 1)
                nc.scalar.activation(fs[u % 3][:, 0:w], fs[u % 3][:, 0:w], ACT.Exp, bias=fnm[:, u:u + 1],
                                     accum_out=frs[:, u:u + 1]).then_inc(p_done, 1)

            def f_pt(u):
                w = P * (u % ST + 1)
                act.wait_ge(pt_ps, u + 1)
                if u >= 2:
                    act.wait_ge(o_ps, u - 1)
                nc.scalar.activation(fpT[u % 2][:, 0:w], PS[2 + u % 2][:, 0:w], ACT.Copy).then_inc(pt_act, 1)

            def kv_evac(g):
                if g == XKV0:
                    act.wait_ge(ho_step, 2 * HP)
                k = g - XKV0
                dst = xkT[:, k] if k < DC else xv[:, (k - DC) % MT, 512 * ((k - DC) // MT):512 * ((k - DC) // MT) + 512]
                act.wait_ge(proj, g + 1)
                nc.scalar.activation(dst, PS[bank_of(g)][:, 0:dst.shape[-1]], ACT.Copy).then_inc(proj_out, 1)

            for u in range(FH * ST + LAG):
                if u < FH * ST:
                    f_exp(u)
                if u >= LAG and (u - LAG) % 2 == 1:
                    f_pt(u - LAG)
                if u - 1 in KV_AT:
                    kv_evac(XKV0 + KV_AT.index(u - 1))

            for t in range(ST):
                act.wait_ge(x1_done, 2 * t + 2)
                square(act, 2, t, x_sb, junk[:, t % 2])
            kv_evac(XQ0 - 1)
            for c in range(DC):
                g = XQ0 + c
                act.wait_ge(proj, g + 1)
                nc.scalar.activation(xqT[:, c], PS[bank_of(g)][:, :], ACT.Copy).then_inc(proj_out, 1)

            def x_exp(u):
                h, t = divmod(u, ST)
                act.wait_ge(xm_done, u + 1)
                if h >= 2:
                    act.wait_ge(xpt_ps, 2 * (h - 1))
                nc.scalar.activation(xp[:, h % 2, t, :], PS[u % 2][:, 0:M], ACT.Exp, bias=fnm[:, u:u + 1],
                                     scale=(D // XH) ** -0.5, accum_out=frs[:, u:u + 1]).then_inc(xe_done, 1)

            def x_out(h):
                for n in range(2):
                    g = 2 * h + n
                    act.wait_ge(xo_ps, g + 1)
                    nc.scalar.activation(xoT[:, g], PS[6 + n][:, :], ACT.Copy).then_inc(xo_sb, 1)

            for h in range(XH + 1):
                if h < XH:
                    for t in range(ST):
                        x_exp(h * ST + t)
                if h >= 1:
                    x_out(h - 1)
            experts_act(act)

        def mean_square(dve, stage, t):
            n = NORM0[stage] + t
            dve.wait_ge(sq_done, n + 1)
            nc.vector.tensor_scalar(ss[:, n:n + 1], ss[:, n:n + 1], 1.0 / D, EPS, ALU.mult, ALU.add).then_inc(ms_done, 1)

        def normed(dve, stage, t, src, dst):
            mean_square(dve, stage, t)
            scaled(dve, stage, t, src, dst)

        def scaled(dve, stage, t, src, dst):
            n = NORM0[stage] + t
            dve.wait_ge(rstd_done, n + 1)
            nc.vector.tensor_scalar(dst[:, t, :], src[:, t, :], rstd[:, n:n + 1], None, ALU.mult).then_inc(n_done, 1)

        def turn_evac(dve, stage, t, k, bank, dst, r0):
            dve.wait_ge(turned, TURN0[stage] + 2 * t + k + 1)
            nc.vector.tensor_tensor(dst[:, 4 * k:4 * k + 4, t * P:(t + 1) * P], bank[:, :].rearrange("p (c t) -> p c t", c=4),
                                    pc[:, r0 + 4 * k:r0 + 4 * k + 4].rearrange("p (c o) -> p c o", o=1).to_broadcast([P, 4, P]),
                                    ALU.mult).then_inc(turn_sb, 1)

        def turn_tile(dve, stage, t, dst, r0):
            for k in range(2):
                turn_evac(dve, stage, t, k, PS[4 + (2 * t + k) % 4], dst, r0)

        def experts_dve(dve):
            steps = [0]

            def link(ins):
                steps[0] += 1
                ins.then_inc(route, 1)
                dve.wait_ge(route, steps[0])

            def over_last(ap, k):
                return ap.rearrange("p (a o) -> p a o", o=1).to_broadcast([P, ST, k])

            def across_rows(ap):
                return ap.rearrange("p t (o j) -> p t o j", o=1).to_broadcast([P, ST, 4, 4])

            def across_cols(ap):
                return ap.rearrange("p t (i o) -> p t i o", o=1).to_broadcast([P, ST, 4, 4])

            def rank(val, dst):
                link(nc.vector.tensor_tensor(beats, across_rows(val), across_cols(val), ALU.is_gt))
                link(nc.vector.tensor_tensor(ties, across_rows(val), across_cols(val), ALU.is_equal))
                low = lower.rearrange("p (o i) j -> p o i j", o=1).to_broadcast([P, ST, 4, 4])
                link(nc.vector.tensor_tensor(ties, ties, low, ALU.mult))
                link(nc.vector.tensor_tensor(beats, beats, ties, ALU.add))
                link(nc.vector.tensor_reduce(dst, beats, AX_X, ALU.add))

            dve.wait_ge(logits_ps, 1)
            dve.wait_ge(router_in, 16 * 4)
            dve.wait_ge(router_const, 7)
            link(nc.vector.tensor_tensor(logits, PS[0][:, 0:ST * (NG + EX)].rearrange("p (t n) -> p t n", t=ST),
                                         rbias.rearrange("p (o n) -> p o n", o=1).to_broadcast([P, ST, NG + EX]), ALU.add))
            gl = logits[:, :, 0:NG]
            el = logits[:, :, NG:].rearrange("p t (g e) -> p t g e", g=NG)
            link(nc.vector.tensor_reduce(gtop, gl, AX_X, ALU.max))
            nc.vector.tensor_tensor(gexp, gl, over_last(gtop, NG), ALU.subtract).then_inc(soft_in, 1)
            rank(gl, grank)
            link(nc.vector.tensor_scalar(ghot, grank, 0.0, None, ALU.is_equal))
            link(nc.vector.tensor_tensor(spread, el, across_cols(ghot), ALU.mult))
            link(nc.vector.tensor_reduce(esel, spread.rearrange("p t g e -> p t e g"), AX_X, ALU.add))
            link(nc.vector.tensor_reduce(etop, esel, AX_X, ALU.max))
            nc.vector.tensor_tensor(eexp, esel, over_last(etop, NE), ALU.subtract).then_inc(soft_in, 1)
            rank(esel, erank)
            link(nc.vector.tensor_scalar(ehot, erank, 2.0, None, ALU.is_lt))
            link(nc.vector.tensor_tensor(picked.rearrange("p t (g e) -> p t g e", g=NG), across_cols(ghot),
                                         across_rows(ehot), ALU.mult))
            nc.vector.tensor_copy(pickedb, picked).then_inc(picked_done, 1)
            dve.wait_ge(pos_ps, 1)
            link(nc.vector.tensor_copy(pos, PS[1][:, 0:ST * EX].rearrange("p (t e) -> p t e", t=ST)))
            link(nc.vector.scalar_tensor_tensor(out=posm, in0=picked, scalar=-4096.0, in1=pos, op0=ALU.mult, op1=ALU.add))
            link(nc.vector.tensor_scalar(posm16, posm, 4096.0, None, ALU.add))

            def pick_rows(t, e0, e1):
                nc.vector.tensor_tensor(pick[:, t, e0:e1], ranks16.rearrange("p (o r) -> p o r", o=1).to_broadcast([P, e1 - e0, P]),
                                        posm16[:, t, e0:e1].rearrange("p (e o) -> p e o", o=1).to_broadcast([P, e1 - e0, P]),
                                        ALU.is_equal).then_inc(pick_done, 1)

            for t in range(ST):
                pick_rows(t, 0, EARLY)
            dve.wait_ge(token_ps, 1)
            nc.vector.tensor_copy(token_of[:, 0:EARLY], PS[3][:, 0:EARLY]).then_inc(token_done, 1)
            link(nc.vector.tensor_reduce(most, PS[2][:, 0:EX], AX_X, ALU.max))
            nc.vector.tensor_scalar(over, most, float(P), None, ALU.is_gt).then_inc(over_done, 1)
            for t in range(2):
                pick_rows(t, EARLY, EX)

            def combine():
                dve.wait_ge(soft_out, 1)
                link(nc.vector.tensor_reduce(gsum, gexp, AX_X, ALU.add))
                link(nc.vector.reciprocal(gsum, gsum))
                dve.wait_ge(soft_out, 2)
                link(nc.vector.tensor_tensor(eexp, eexp, ehot, ALU.mult))
                link(nc.vector.tensor_reduce(esum, eexp, AX_X, ALU.add))
                link(nc.vector.reciprocal(esum, esum))
                link(nc.vector.tensor_tensor(eexp, eexp, over_last(esum, NE), ALU.mult))
                link(nc.vector.tensor_tensor(eexp, eexp, over_last(gsum, NE), ALU.mult))
                link(nc.vector.tensor_tensor(weight.rearrange("p t (g e) -> p t g e", g=NG), across_cols(ghot),
                                             across_rows(eexp), ALU.mult))
                link(nc.vector.tensor_scalar(part, pos, float(P), None, ALU.is_ge))
                for k in range(2, ST):
                    link(nc.vector.scalar_tensor_tensor(out=part, in0=pos, scalar=float(k * P), in1=part, op0=ALU.is_ge, op1=ALU.add))
                link(nc.vector.scalar_tensor_tensor(out=slot, in0=part, scalar=float((EX - 1) * P), in1=pos, op0=ALU.mult, op1=ALU.add))
                link(nc.vector.tensor_tensor(slot, slot, ebase.rearrange("p (o e) -> p o e", o=1).to_broadcast([P, ST, EX]), ALU.add))
                link(nc.vector.tensor_tensor(slot, slot, picked, ALU.mult))
                link(nc.vector.tensor_reduce(stop_, slot, AX_X, ALU.max))
                link(nc.vector.tensor_reduce(ssum_, slot, AX_X, ALU.add))
                nc.vector.tensor_copy(slot2, stop_).then_inc(slots_done, 1)
                nc.vector.tensor_tensor(slot1, ssum_, stop_, ALU.subtract).then_inc(slots_done, 1)
                link(nc.vector.tensor_tensor(part, slot, over_last(stop_, EX), ALU.is_equal))
                link(nc.vector.tensor_tensor(part, part, weight, ALU.mult))
                link(nc.vector.tensor_reduce(w2nd, part, AX_X, ALU.add))
                link(nc.vector.tensor_tensor(part, slot, over_last(stop_, EX), ALU.not_equal))
                link(nc.vector.tensor_tensor(part, part, weight, ALU.mult))
                link(nc.vector.tensor_reduce(w1st, part, AX_X, ALU.add))

            gains = pc[:, R_FFN:R_FFN + DC]

            def turned_rows(e, b, first):
                if not first:
                    dve.wait_ge(gu_ps, e - 1)
                for k in range(2):
                    dve.wait_ge(xt_ps, 2 * e + k + 1)
                    nc.vector.tensor_tensor(xgT[:, b, 4 * k:4 * k + 4, :], PS[k][:, :].rearrange("p (c t) -> p c t", c=4),
                                            gains[:, 4 * k:4 * k + 4].rearrange("p (c o) -> p c o", o=1).to_broadcast([P, 4, P]),
                                            ALU.mult).then_inc(xt_sb, 1)

            def hidden(e, b, first):
                dve.wait_ge(silu_done, e + 1)
                if not first:
                    dve.wait_ge(ht_ps, e - 1)
                nc.vector.tensor_tensor(hid[:, b], sg[:, b], PS[2 + b][:, FF:2 * FF], ALU.mult).then_inc(hid_done, 1)

            def y_half(e, b, first):
                dve.wait_ge(y_ps, 2 * e + 2)
                if not first:
                    dve.wait_ge(y_stored[b], 16 * ((e + (-b)) // 2))
                nc.vector.tensor_copy(ysb[:, b, 512:1024], PS[6][:, :]).then_inc(y_dve, 1)

            def step(e, j, start, last=False):
                hidden(e, j % 2, start and j < 2)
                if not last:
                    turned_rows(e + 1, (j + 1) % 2, start and j == 0)
                if not (start and j == 0):
                    y_half(e - 1, (j + 1) % 2, start and j < 3)
                if start and j == 0:
                    combine()

            turned_rows(0, 0, True)
            for t in range(2, ST):
                pick_rows(t, EARLY, EX)
            link(nc.vector.tensor_scalar(posm, posm, 4096.0, None, ALU.add))
            dve.wait_ge(token_ps, 2)
            nc.vector.tensor_copy(token_of[:, EARLY:EX], PS[4][:, EARLY:EX]).then_inc(token_done, 1)
            for j in range(SLOTS):
                step(j, j, True)
            with dve.Fori(1, EX // SLOTS - 1) as i:
                for j in range(SLOTS):
                    step(i * SLOTS + j, j, False)
            for j in range(SLOTS):
                step(EX - SLOTS + j, j, False, last=j == SLOTS - 1)
            y_half(EX - 1, 1, False)

            with dve.If(dve.value_load(over[0:1, 0:1]) > 0):
                dve.wait_ge(gu_ps, EX)
                dve.wait_ge(ht_ps, EX)
                with dve.Fori(0, ST - 1) as q:
                    nc.vector.tensor_scalar(posm, posm, -float(P), None, ALU.add).then_inc(ov_pos, 1)
                    with dve.Fori(0, EX) as e:
                        k = q * EX + e
                        dve.wait_ge(ov_pos, q + 1)
                        for t in range(ST):
                            nc.vector.tensor_scalar(ov_pick[:, t], ranks, posm[:, t, bass.ds(e, 1)], None,
                                                    ALU.is_equal).then_inc(ov_picked, 1)
                        dve.wait_ge(ov_token_ps, k + 1)
                        nc.vector.tensor_copy(ov_token, PS[3][:, 0:1]).then_inc(ov_token_sb, 1)
                        for n in range(2):
                            dve.wait_ge(ov_xt_ps, 2 * k + n + 1)
                            nc.vector.tensor_tensor(xgT[:, 0, 4 * n:4 * n + 4, :], PS[n][:, :].rearrange("p (c t) -> p c t", c=4),
                                                    gains[:, 4 * n:4 * n + 4].rearrange("p (c o) -> p c o", o=1).to_broadcast([P, 4, P]),
                                                    ALU.mult).then_inc(ov_xt_sb, 1)
                        dve.wait_ge(ov_silu, k + 1)
                        nc.vector.tensor_tensor(hid[:, 0], sg[:, 0], PS[2][:, FF:2 * FF], ALU.mult).then_inc(ov_hid, 1)
                        dve.wait_ge(ov_stored, 16 * k + 16)
            with dve.Else():
                pass
            def add_row(k, t, w):
                dve.wait_ge(fin_in[t][k], 16)
                if k:
                    dve.wait_ge(fin_sum, t + 1)
                nc.vector.scalar_tensor_tensor(out=x_sb[:, t, :], in0=ygath[:, t, k, :], scalar=w[:, t:t + 1],
                                               in1=x_sb[:, t, :], op0=ALU.mult, op1=ALU.add).then_inc(fin_sum, 1)

            for t in range(ST):
                add_row(0, t, w1st)
            dve.wait_ge(router_in, 16 * 5)
            for t in range(ST + 2):
                if t < ST:
                    add_row(1, t, w2nd)
                if 1 <= t <= ST:
                    f = NORM0[3] + ST + t - 1
                    dve.wait_ge(fin_sq, t)
                    nc.vector.tensor_scalar(ss[:, f:f + 1], ss[:, f:f + 1], 1.0 / D, EPS, ALU.mult, ALU.add).then_inc(fin_ms, 1)
                if t >= 2:
                    u = t - 2
                    dve.wait_ge(fin_root, u + 1)
                    nc.vector.scalar_tensor_tensor(out=n_sb[:, u, :], in0=x_sb[:, u, :], scalar=rstd[:, NORM0[3] + ST + u:NORM0[3] + ST + u + 1],
                                                   in1=fgain, op0=ALU.mult, op1=ALU.mult).then_inc(fin_out, 1)

        @block.vector
        def _(dve):
            nc.vector.memset(half64[:, :], 0.0).then_inc(half_done, 1)
            dve.wait_ge(half_done, 1)
            nc.vector.memset(half64[0:64, 0:64], 1.0 / 64).then_inc(half_done, 1)
            nc.vector.memset(half64[64:128, 64:128], 1.0 / 64).then_inc(half_done, 1)
            for t in range(ST + 1):
                if t < ST:
                    normed(dve, 0, t, x_sb, n_sb)
                if t == 0:
                    dve.wait_ge(pcol_ps, 1)
                    nc.vector.tensor_copy(pc[:, 0:DC], PS[0][:, 0:DC]).then_inc(pcol, 1)
                    dve.wait_ge(pcol, 1)
                if t >= 1:
                    turn_tile(dve, 0, t - 1, hT, R_MIX)

            dve.wait_ge(pcol_ps, 2)
            nc.vector.tensor_copy(pc[:, DC:NR], PS[1][:, DC:NR]).then_inc(pcol, 1)
            dve.wait_ge(pcol, 2)
            lg = pc[:, R_LB:R_LB + HP]
            nc.vector.tensor_tensor(lbv[:, 0:2], lg, lg, ALU.subtract).then_inc(lb_step, 1)
            dve.wait_ge(lb_step, 1)
            nc.vector.tensor_tensor(lbv[:, 2:4], lbv[:, 0:2], lbv[:, 0:2], ALU.subtract).then_inc(lb_step, 1)
            dve.wait_ge(lb_step, 2)
            nc.vector.tensor_scalar(lbv[:, 4:6], lbv[:, 2:4], -1.0, 1.0, ALU.mult, ALU.add).then_inc(lb_step, 1)

            for c in range(2):
                dve.wait_ge(proj_out, 3 + c)
                nc.vector.tensor_tensor(cuT[:, c], cuT[:, c], cgT[:, c], ALU.mult).then_inc(conv_a, 1)
            def conv(c, w0, w1):
                y, a = cgT[:, c], cuT[:, c]
                for w in range(w0, w1):
                    s = w
                    r = R_CW + 2 * (CW - 1 - s) + c
                    if s == 0:
                        dve.wait_ge(conv_a, c + 1)
                        nc.vector.tensor_scalar(y, a, pc[:, r:r + 1], pc[:, R_CB + c:R_CB + c + 1], ALU.mult,
                                                ALU.add).then_inc(conv_y, 1)
                    else:
                        dve.wait_ge(conv_y, c * CW + s)
                        nc.vector.scalar_tensor_tensor(out=y[:, s:S], in0=a[:, 0:S - s], scalar=pc[:, r:r + 1],
                                                       in1=y[:, s:S], op0=ALU.mult, op1=ALU.add).then_inc(conv_y, 1)

            taps = [(c, w) for c in range(2) for w in range(CW)]

            def conv_some(n):
                for c, w in taps[:n]:
                    conv(c, w, w + 1)
                del taps[:n]

            conv_some(26)
            dve.wait_ge(lb_step, 3)
            for p in range(HP):
                dve.wait_ge(proj_out, 7 + p)
                nc.vector.tensor_scalar(hfT[:, p], hfT[:, p], lbv[:, 4 + p:5 + p], lbv[:, 2 + p:3 + p], ALU.mult,
                                        ALU.add).then_inc(hf_done, 1)
                dve.wait_ge(hf_done, 2 * p + 1)
                nc.vector.tensor_scalar(hk[:, p], hfT[:, p], -1.0, 1.0, ALU.mult, ALU.add).then_inc(hf_done, 1)

            for p in range(HP):
                dve.wait_ge(hg_log, p + 1)
                if p == 0:
                    dve.wait_ge(consts, 8)
                nc.vector.tensor_tensor_scan(hb[:, p], scanmask[:, :], hgl[:, p], 0.0, ALU.mult, ALU.add).then_inc(hb_done, 1)
                dve.wait_ge(hb_done, p + 1)
                b3 = hb[:, p].rearrange("p (n j) -> p n j", j=CHUNK)
                nc.vector.tensor_tensor(hd1[:, p].rearrange("p (n j) -> p n j", j=CHUNK), b3,
                                        b3[:, :, CHUNK // 2:CHUNK // 2 + 1].to_broadcast([P, NCH, CHUNK]),
                                        ALU.subtract).then_inc(hd_done, 1)
                nc.vector.tensor_tensor(hgl[:, p].rearrange("p (n j) -> p n j", j=CHUNK), b3,
                                        b3[:, :, CHUNK - 1:CHUNK].to_broadcast([P, NCH, CHUNK]),
                                        ALU.subtract).then_inc(hd_done, 1)
            conv_some(14)
            dve.wait_ge(proj_out, 13)
            nc.vector.memset(ones8[:, :], 1.0).then_inc(ones_done, 1)
            nc.vector.tensor_scalar(lfa[:, :], lfa[:, :], fbias[:, 0:1], None, ALU.add).then_inc(lf_dve, 1)
            dve.wait_ge(lf_dve, 1)
            nc.vector.scalar_tensor_tensor(out=lfb[:, :], in0=lfa[:, :], scalar=-1.0, in1=lfa[:, :], op0=ALU.mult,
                                           op1=ALU.max).then_inc(lf_dve, 1)
            dve.wait_ge(lf_dve, 2)
            nc.vector.tensor_scalar(lfa[:, :], lfa[:, :], 0.0, None, ALU.min).then_inc(lf_dve, 1)
            dve.wait_ge(he_done, 4 * HP)
            nc.vector.memset(attm.rearrange("p a b c -> p (a b c)"), 0.0).then_inc(att_zero, 1)
            nc.vector.memset(states[:, 0, :], 0.0).then_inc(state_step, 1)
            dve.wait_ge(lf_act, 2)
            nc.vector.tensor_tensor(lfb[:, :], lfb[:, :], lfa[:, :], ALU.subtract).then_inc(lf_dve, 1)
            dve.wait_ge(lf_dve, 4)
            dve.wait_ge(ones_done, 1)
            nc.vector.tensor_tensor_scan(lfa[:, :], ones8[:, :], lfb[:, :], 0.0, ALU.mult, ALU.add).then_inc(lf_dve, 1)

            conv_some(len(taps))

            def states_of(p, t):
                i = p * ST + t
                dve.wait_ge(u_done, i + 1)
                for n in range(CPT):
                    k = t * CPT + n
                    dve.wait_ge(state_step, 1 + i * CPT + n)
                    nc.vector.scalar_tensor_tensor(
                        out=states[:, k + 1, :], in0=states[:, k, :],
                        scalar=he4[:, p, k * CHUNK + CHUNK - 1:k * CHUNK + CHUNK],
                        in1=PS[2 + i % 2][:, n * HD:(n + 1) * HD], op0=ALU.mult, op1=ALU.add).then_inc(state_step, 1)

            def att_mask(p):
                for a in range(2):
                    h = 2 * p + a
                    dve.wait_ge(att_ps, h + 1)
                    nc.vector.copy_predicated(attm[:, h], chunkmask[:, :].rearrange("p (o t) -> p o t", o=1).to_broadcast([P, ST, P]),
                                              PS[4 + a][:, :].rearrange("p (t s) -> p t s", t=ST)).then_inc(att_done, 1)

            dve.wait_ge(att_zero, 1)
            att_mask(0)
            for t in range(ST):
                states_of(0, t)
            att_mask(1)
            for c in range(2):
                dve.wait_ge(cmean, c + 1)
                nc.vector.tensor_tensor(cuT[:, c], cgT[:, c], PS[4 + c][:, :], ALU.subtract).then_inc(cdev, 1)
                dve.wait_ge(cdev, 2 * c + 1)
                nc.vector.tensor_tensor(cgT[:, c], cuT[:, c], cuT[:, c], ALU.mult).then_inc(cdev, 1)
            dve.wait_ge(ho_ps, 1)
            for t in range(ST):
                states_of(1, t)

            for c in range(2):
                dve.wait_ge(crs, c + 1)
                nc.vector.tensor_tensor(cuT[:, c], cuT[:, c], croot[c], ALU.mult).then_inc(cz, 1)
            for p in range(HP):
                dve.wait_ge(ho_sb, p + 1)
                nc.vector.tensor_tensor(he3[:, p], hob[p], hob[p], ALU.mult).then_inc(ho_sq, 1)
            for t in range(MT):
                normed(dve, 1, t, mem_sb, mem_sb)
            for p in range(HP):
                dve.wait_ge(ho_rs, p + 1)
                nc.vector.scalar_tensor_tensor(out=hob[p], in0=hob[p], scalar=pc[:, R_HG + p:R_HG + p + 1],
                                               in1=hrb[p], op0=ALU.mult, op1=ALU.mult).then_inc(ho_step, 1)
                dve.wait_ge(ho_step, 2 * p + 1)
                nc.vector.tensor_tensor(catT[:, 4 + p], hob[p], hgT[:, p], ALU.mult).then_inc(ho_step, 1)

            for k in range(2 * MT):
                turn_evac(dve, 1, k // 2, k % 2, PS[6 + k % 2], memT, R_MEM)

            def f_scores(u):
                h, i = divmod(u, ST)
                w = P * (i + 1)
                if i == 0:
                    dve.wait_ge(negc_sb, h + 1)
                dve.wait_ge(qk_done, u + 1)
                if u >= 3:
                    dve.wait_ge(pt_ps, u - 2)
                nc.vector.tensor_tensor_reduce(fs[u % 3][:, 0:w], PS[u % 2][:, 0:w], fnegc[h % 2][:, 0:w], 1.0, LOWEST,
                                               ALU.add, ALU.max, fmx[:, u:u + 1]).then_inc(s_done, 1)
                dve.wait_ge(s_done, u + 1)
                nc.vector.tensor_scalar(fnm[:, u:u + 1], fmx[:, u:u + 1], -1.0, None, ALU.mult).then_inc(m_done, 1)

            def f_pt(u):
                w = P * (u % ST + 1)
                dve.wait_ge(pt_ps, u + 1)
                if u >= 2:
                    dve.wait_ge(o_ps, u - 1)
                nc.vector.tensor_copy(fpT[u % 2][:, 0:w], PS[2 + u % 2][:, 0:w]).then_inc(pt_dve, 1)

            def f_out(u):
                h, i = divmod(u, ST)
                dve.wait_ge(p_done, u + 1)
                nc.vector.reciprocal(frr[:, u:u + 1], frs[:, u:u + 1]).then_inc(f_step, 1)
                dve.wait_ge(f_step, u + 1)
                dve.wait_ge(o_ps, u + 1)
                nc.vector.tensor_scalar(fo[:, i, h * FD:(h + 1) * FD], PS[4 + u % 2][:, 0:FD], frr[:, u:u + 1], None,
                                        ALU.mult).then_inc(o_sb, 1)

            def f_square(h):
                dve.wait_ge(o_sb, ST * (h + 1))
                if h:
                    dve.wait_ge(f_ms, h)
                src = fo[:, :, h * FD:(h + 1) * FD]
                nc.vector.tensor_tensor(fsq, src, src, ALU.mult).then_inc(f_sq_step, 1)
                dve.wait_ge(f_sq_step, 2 * h + 1)
                nc.vector.tensor_reduce(fss[:, 4 * h:4 * h + 4], fsq, AX_X, ALU.add).then_inc(f_sq_step, 1)
                dve.wait_ge(f_sq_step, 2 * h + 2)
                nc.vector.tensor_scalar(fss[:, 4 * h:4 * h + 4], fss[:, 4 * h:4 * h + 4], 1.0 / FD, EPS, ALU.mult,
                                        ALU.add).then_inc(f_ms, 1)

            def f_norm(h):
                dve.wait_ge(f_rstd, h + 1)
                src = fo[:, :, h * FD:(h + 1) * FD]
                nc.vector.tensor_tensor(src, src, frstd[:, 4 * h:4 * h + 4].rearrange("p (t o) -> p t o", o=1).to_broadcast([P, ST, FD]),
                                        ALU.mult).then_inc(f_normed, 1)

            def f_turned(n, c, bank):
                dve.wait_ge(fo_turned, n + 1)
                nc.vector.tensor_scalar(catT[:, c], bank[:, :], pc[:, R_FOX + c:R_FOX + c + 1], None,
                                        ALU.mult).then_inc(cat_out, 1)

            def f_negc(h):
                dve.wait_ge(negc_ps, h + 1)
                nc.vector.tensor_copy(fnegc[h % 2], PS[6][:, :]).then_inc(negc_sb, 1)

            f_negc(0)
            for u in range(FH * ST + LAG + 1):
                if u < FH * ST:
                    f_scores(u)
                if LAG <= u < FH * ST + LAG and (u - LAG) % 2 == 0:
                    f_pt(u - LAG)
                if u > LAG:
                    done = u - LAG - 1
                    f_out(done)
                    if done % ST == ST - 1:
                        h = done // ST
                        f_square(h)
                        if h >= 1:
                            f_norm(h - 1)
                if u % ST == 2 and u // ST + 1 < FH:
                    f_negc(u // ST + 1)
                if u - 1 in FO_AT:
                    f_turned(list(FO_AT).index(u - 1), FO_AT[u - 1], PS[7])
            f_norm(FH - 1)
            f_turned(3, 3, PS[6])

            def residual(base, stage, r0):
                for t in range(ST + 1):
                    if t < ST:
                        for n in range(2):
                            dve.wait_ge(wout_ps, base + 2 * t + n + 1)
                            xs = x_sb[:, t, 512 * n:512 * n + 512]
                            nc.vector.tensor_tensor(xs, xs, PS[(2 * t + n) % 4][:, :], ALU.add).then_inc(x1_done, 1)
                    for k in range(2):
                        if t >= 1:
                            turn_evac(dve, stage, t - 1, k, PS[4 + (2 * (t - 1) + k) % 4], hT, r0)
                        if k == 0 and t < ST:
                            mean_square(dve, stage, t)
                    if t < ST:
                        scaled(dve, stage, t, x_sb, nA)

            residual(0, 2, R_XATT)

            def x_max(u):
                dve.wait_ge(xs_ps, u + 1)
                nc.vector.tensor_reduce(fmx[:, u:u + 1], PS[u % 2][:, 0:M], AX_X, ALU.max).then_inc(xs_step, 1)
                dve.wait_ge(xs_step, u + 1)
                nc.vector.tensor_scalar(fnm[:, u:u + 1], fmx[:, u:u + 1], -((D // XH) ** -0.5), None,
                                        ALU.mult).then_inc(xm_done, 1)

            def x_norm(u):
                dve.wait_ge(xe_done, u + 1)
                nc.vector.reciprocal(frr[:, u:u + 1], frs[:, u:u + 1]).then_inc(xr_done, 1)
                dve.wait_ge(xr_done, u + 1)
                pr = xp[:, u // ST % 2, u % ST, :]
                nc.vector.tensor_scalar(pr, pr, frr[:, u:u + 1], None, ALU.mult).then_inc(xn_done, 1)

            def x_pt(h):
                for m in range(2):
                    g = 2 * h + m
                    dve.wait_ge(xpt_ps, g + 1)
                    if h >= 2:
                        dve.wait_ge(xo_ps, 2 * (h - 1))
                    nc.vector.tensor_copy(xpT[:, g % 4], PS[4 + m][:, :]).then_inc(xpt_sb, 1)

            for h in range(XH + 1):
                for t in range(ST):
                    if h < XH:
                        x_max(h * ST + t)
                        if t >= 1:
                            x_norm(h * ST + t - 1)
                    if t == 1 and h:
                        x_pt(h - 1)
                if h < XH:
                    x_norm(h * ST + ST - 1)
            residual(8, 3, R_FFN)
            experts_dve(dve)

        def turn_group(pe, stage, t, k, bank, src):
            pe.wait_ge(n_done, NORM0[stage] + t + 1)
            for c in range(4):
                mm = nc.tensor.transpose(bank[:, c * P:(c + 1) * P], src[:, t, (4 * k + c) * P:(4 * k + c + 1) * P], identf[:, :])
            mm.then_inc(turned, 1)

        def experts_pe(pe):
            pe.wait_ge(x1_done, 16)
            for t in range(ST):
                pe.wait_ge(lgt_sb, t + 1)
                mm = nc.tensor.transpose(PS[0][:, t * (NG + EX):(t + 1) * (NG + EX)], lgT[:, t * P:(t + 1) * P],
                                         identf[0:NG + EX, 0:NG + EX])
            mm.then_inc(logits_ps, 1)
            pe.wait_ge(picked_done, 1)
            pe.wait_ge(router_const, 7)
            for t in range(ST):
                for u in range(t + 1):
                    nc.tensor.matmul(PS[1][:, t * EX:(t + 1) * EX], onesb if u < t else before, pickedb[:, u],
                                     start=u == 0, stop=u == t)
            for u in range(ST):
                mm = nc.tensor.matmul(PS[2][:, 0:EX], onesb, pickedb[:, u], start=u == 0, stop=u == ST - 1)
            mm.then_inc(pos_ps, 1)
            def tokens_of(bank, n0, t, e0, e1):
                pe.wait_ge(pick_done, n0 + t + 1)
                for e in range(e0, e1):
                    mm = nc.tensor.matmul(bank[:, e:e + 1], pick[:, t, e, :], tokid[:, t:t + 1], start=t == 0 and e == e0,
                                          stop=t == ST - 1 and e == e1 - 1, skip_group_check=True)
                if t == ST - 1:
                    mm.then_inc(token_ps, 1)

            for t in range(ST):
                tokens_of(PS[3], 0, t, 0, EARLY)

            def turn_rows(src, b, done):
                for k in range(2):
                    for c in range(4):
                        mm = nc.tensor.transpose(PS[k][:, c * P:(c + 1) * P], src[:, b, (4 * k + c) * P:(4 * k + c + 1) * P], identf[:, :])
                    mm.then_inc(done, 1)

            def turn_hidden(b, done):
                for k in range(2):
                    mm = nc.tensor.transpose(PS[4][:, k * P:(k + 1) * P], hid[:, b, k * P:(k + 1) * P], identf[:, :])
                mm.then_inc(done, 1)

            def gate_up(b, s, bank, done):
                for c in range(DC):
                    mm = nc.tensor.matmul(bank[:, :], xgT[:, b, c, :], W[:, s, c, :], start=c == 0, stop=c == DC - 1)
                mm.then_inc(done, 1)

            def down(b, s, n, done):
                for k in range(2):
                    mm = nc.tensor.matmul(PS[5 + n][:, :], hidT[:, b, k, :], Dn[:, s, k, 512 * n:512 * n + 512],
                                          start=k == 0, stop=k == 1)
                mm.then_inc(done, 1)

            def turn_expert(e, b, start):
                pe.wait_ge(xg_in[b], 16 * ((e + (2 - b)) // 2))
                if not start:
                    pe.wait_ge(xt_sb, 2 * e)
                turn_rows(xg, b, xt_ps)

            def step(e, j, turn_, start, last=False):
                b = j % 2
                pe.wait_ge(xt_sb, 2 * e + 2)
                gate_up_loaded(pe, j, turn_)
                gate_up(b, j, PS[2 + b], gu_ps)
                if start and j == 0:
                    for t in range(2, ST):
                        tokens_of(PS[4], ST, t, EARLY, EX)
                if not last:
                    turn_expert(e + 1, 1 - b, False)
                if not (start and j == 0):
                    down_expert(e - 1, 1 - b, (j - 1) % SLOTS, turn_ + (0 if j == 0 else 1), start and j == 1)
                pe.wait_ge(hid_done, e + 1)
                if not (start and j == 0):
                    pe.wait_ge(ht_sb, e)
                turn_hidden(b, ht_ps)

            def down_expert(e, b, s, turns, first):
                pe.wait_ge(ht_sb, e + 1)
                pe.wait_ge(dn_loaded[s], 16 * turns)
                for n, left in enumerate((y_act, y_dve)):
                    if not first:
                        pe.wait_ge(left, e)
                    down(b, s, n, y_ps)

            for t in range(2):
                tokens_of(PS[4], ST, t, EARLY, EX)
            pe.wait_ge(over_done, 1)
            turn_expert(0, 0, True)
            for j in range(SLOTS):
                step(j, j, 0, True)
            with pe.Fori(1, EX // SLOTS - 1) as i:
                for j in range(SLOTS):
                    step(i * SLOTS + j, j, i, False)
            for j in range(SLOTS):
                step(EX - SLOTS + j, j, EX // SLOTS - 1, False, last=j == SLOTS - 1)
            down_expert(EX - 1, 1, SLOTS - 1, EX // SLOTS, False)

            pe.wait_ge(over_done, 1)
            with pe.If(pe.value_load(over[0:1, 0:1]) > 0):
                pe.wait_ge(y_act, EX)
                pe.wait_ge(y_dve, EX)
                with pe.Fori(0, (ST - 1) * EX) as k:
                    pe.wait_ge(ov_picked, ST * k + ST)
                    for t in range(ST):
                        mm = nc.tensor.matmul(PS[3][:, 0:1], ov_pick[:, t], tokid[:, t:t + 1], start=t == 0, stop=t == ST - 1)
                    mm.then_inc(ov_token_ps, 1)
                    pe.wait_ge(ov_xg, 16 * k + 16)
                    turn_rows(xg, 0, ov_xt_ps)
                    pe.wait_ge(ov_xt_sb, 2 * k + 2)
                    pe.wait_ge(ov_w, 48 * k + 48)
                    gate_up(0, 0, PS[2], ov_gu)
                    pe.wait_ge(ov_hid, k + 1)
                    turn_hidden(0, ov_ht_ps)
                    pe.wait_ge(ov_ht_sb, k + 1)
                    for n in range(2):
                        down(0, 0, n, ov_y_ps)
                    pe.wait_ge(ov_y_sb, 2 * k + 2)
            with pe.Else():
                pass

        @block.tensor
        def _(pe):
            def turn_tile_pe(stage, t, src):
                for k in range(2):
                    i = 2 * t + k
                    if i >= 4:
                        pe.wait_ge(turn_sb, TURN0[stage] + i - 3)
                        if stage == 3 and k == 0:
                            pe.wait_ge(lgt_sb, t - 1)
                    turn_group(pe, stage, t, k, PS[4 + i % 4], src)

            pe.wait_ge(mix_in, 16)
            pe.wait_ge(consts, 5)
            nc.tensor.transpose(PS[0][:, 0:DC], mixrow[:, :], identf[0:DC, 0:DC]).then_inc(pcol_ps, 1)
            for t in range(ST):
                turn_tile_pe(0, t, n_sb)
            pe.wait_ge(params_in, 12 * 16)
            nc.tensor.transpose(PS[1][:, 0:NR], prow[0:NR, :], identf[0:NR, 0:NR]).then_inc(pcol_ps, 1)
            pe.wait_ge(turn_sb, 2 * ST)
            pe.wait_ge(pcol, 2)

            def across(slot, col, w=P, src=None, n=S):
                src = hT if src is None else src

                def f(bank):
                    for c in range(DC):
                        lhs = W[:, slot, c, col:col + w]
                        mm = nc.tensor.matmul(bank[0:w, 0:n], lhs, src[:, c, 0:n], start=c == 0, stop=c == DC - 1)
                    return mm
                return f

            def along(slot, t, col, w, src=None):
                src = hT if src is None else src

                def f(bank):
                    for c in range(DC):
                        mm = nc.tensor.matmul(bank[:, 0:w], src[:, c, t * P:(t + 1) * P], W[:, slot, c, col:col + w],
                                              start=c == 0, stop=c == DC - 1)
                    return mm
                return f

            g = 0

            def run(fs_, g, n_load):
                loaded(pe, n_load)
                for f in fs_:
                    bank_free(pe, g)
                    mm = f(PS[bank_of(g)])
                    mm.then_inc(proj, 1)
                    g += 1
                return g

            g = run([across(0, P * c) for c in range(4)], g, 0)
            g = run([across(1, P * c) for c in range(4)], g, 1)
            def input_and_gates(t):
                def f(bank):
                    for c in range(DC):
                        mm = nc.tensor.matmul(bank[:, 0:IW], hT[:, c, t * P:(t + 1) * P], w_if[:, c, :], start=c == 0, stop=c == DC - 1)
                    return mm
                return f

            def turned_gates(bank):
                pe.wait_ge(ff_sb, ST)
                for t in range(ST):
                    mm = nc.tensor.transpose(bank[0:FH, t * P:(t + 1) * P], fft[:, t, :], identf[:, :])
                return mm

            def hgrn_gate(k):
                def f(bank):
                    for c in range(DC):
                        lhs = w_hg[:, c, k * P:(k + 1) * P] if c < DC - 1 else w_hg_last[k]
                        mm = nc.tensor.matmul(bank[:, :], lhs, hT[:, c, :], start=c == 0, stop=c == DC - 1)
                    return mm
                return f

            pe.wait_ge(hi_in, 4 * 16)
            g = run([input_and_gates(t) for t in range(ST)], g, 2)
            g = run([turned_gates], g, 2)
            g = run([hgrn_gate(k) for k in range(2)], g, 2)
            g = run([across(3, P * c) for c in range(2)], g, 3)
            for p in range(HP):
                pe.wait_ge(hprod, 4 * p + 1)
                for t in range(ST):
                    mm = nc.tensor.transpose(PS[4 + p][:, t * P:(t + 1) * P], he3[:, p, t * P:(t + 1) * P], identf[:, :])
                mm.then_inc(kh_turned, 1)

            def hgrn_att(p):
                if p:
                    pe.wait_ge(att_done, 2)
                else:
                    pe.wait_ge(kh_out, HP)
                pe.wait_ge(hprod, 4 * p + 4)
                for a in range(2):
                    r = slice(64 * a, 64 * a + 64)
                    for t in range(ST):
                        mm = nc.tensor.matmul(PS[4 + a][:, t * P:(t + 1) * P], he2[r, p, t * P:(t + 1) * P],
                                              he1[r, p, t * P:(t + 1) * P], start=True, stop=True)
                    mm.then_inc(att_ps, 1)

            def hgrn_u(i):
                p, t = divmod(i, ST)
                if i == 0:
                    pe.wait_ge(proj_out, 16)
                pe.wait_ge(vexp_done, 2 * i + 2)
                if i >= 2:
                    pe.wait_ge(state_step, 1 + CPT * (i - 1))
                for a in range(2):
                    mm = nc.tensor.matmul(PS[2 + i % 2][64 * a:64 * a + 64, :], khtok[:, p, t, 64 * a:64 * a + 64],
                                          vexp[i % 2][:, a].rearrange("p n v -> p (n v)"), start=True, stop=True)
                mm.then_inc(u_done, 1)

            def hgrn_out(p):
                pe.wait_ge(att_done, 2 * p + 2)
                pe.wait_ge(state_step, 1 + CPT * ST * (p + 1) - 1)
                bank = PS[6 + p]
                for t in range(ST):
                    for a in range(2):
                        r = slice(64 * a, 64 * a + 64)
                        h = 2 * p + a
                        nc.tensor.matmul(bank[r, t * P:(t + 1) * P], hv[:, t, h * HD:(h + 1) * HD], attm[:, h, t, :],
                                         start=t == 0, stop=False, skip_group_check=True)
                for n in range(NCH):
                    for a in range(2):
                        r = slice(64 * a, 64 * a + 64)
                        mm = nc.tensor.matmul(bank[r, n * CHUNK:(n + 1) * CHUNK], states[r, n, :],
                                              hqT[r, p, n * CHUNK:(n + 1) * CHUNK], start=False, stop=n == NCH - 1,
                                              skip_group_check=True)
                mm.then_inc(ho_ps, 1)

            g = run([across(3, P * 2)], g, 3)
            hgrn_att(0)
            g = run([across(3, P * 3)], g, 3)
            hgrn_u(0)
            hgrn_u(1)
            g = run([across(0, 0)], g, 4)
            hgrn_u(2)
            hgrn_u(3)
            hgrn_att(1)
            g = run([across(0, P)], g, 4)
            hgrn_out(0)
            pe.wait_ge(half_done, 3)
            pe.wait_ge(att_done, 4)
            for c in range(2):
                pe.wait_ge(conv_y, CW * (c + 1))
                nc.tensor.matmul(PS[4 + c][:, :], half64[:, :], cgT[:, c], start=True, stop=True).then_inc(cmean, 1)
            hgrn_u(4)
            hgrn_u(5)
            g = run([across(0, P * 2)], g, 4)
            for c in range(2):
                pe.wait_ge(cdev, 2 * c + 2)
                nc.tensor.matmul(PS[4 + c][:, :], half64[:, :], cgT[:, c], start=True, stop=True).then_inc(cvar, 1)
            hgrn_u(6)
            hgrn_u(7)
            g = run([across(0, P * 3)], g, 4)
            g = run([along(1, 0, 0, FW)], g, 5)
            hgrn_out(1)
            g = run([along(1, 1, 0, FW)], g, 5)
            pe.wait_ge(crs, 2)
            for p in range(HP):
                pe.wait_ge(ho_sq, p + 1)
                nc.tensor.matmul(PS[4 + p][:, :], half64[:, :], he3[:, p], start=True, stop=True).then_inc(ho_ms, 1)
            g = run([along(1, 2, 0, FW)], g, 5)
            pe.wait_ge(ho_sb, HP)
            for k in range(2):
                turn_group(pe, 1, 0, k, PS[6 + k], mem_sb)
            g = run([along(1, 3, 0, FW)], g, 5)
            for k in range(2):
                pe.wait_ge(turn_sb, TURN0[1] + k + 1)
                turn_group(pe, 1, 1, k, PS[6 + k], mem_sb)

            def negc(h):
                if h == 0:
                    pe.wait_ge(lf_dve, 5)
                else:
                    pe.wait_ge(negc_sb, h)
                nc.tensor.matmul(PS[6][:, :], identf[0:FH, h:h + 1].to_broadcast([FH, P]), lfa[:, :],
                                 start=True, stop=True).then_inc(negc_ps, 1)

            def qk(u):
                h, i = divmod(u, ST)
                r = slice(64 * (h % 2), 64 * (h % 2) + 64)
                if u >= 2:
                    pe.wait_ge(s_done, u - 1)
                nc.tensor.matmul(PS[u % 2][:, 0:P * (i + 1)], qT[r, h // 2, i * P:(i + 1) * P],
                                 kT[r, h // 2, 0:P * (i + 1)], start=True, stop=False)
                nc.tensor.matmul(PS[u % 2][:, P * i:P * (i + 1)], identb[:, :], causal[:, :], start=False,
                                 stop=True).then_inc(qk_done, 1)

            def pt(u):
                i = u % ST
                pe.wait_ge(p_done, u + 1)
                if u >= 2:
                    pe.wait_ge(pt_dve if u % 2 == 0 else pt_act, u // 2)
                for j in range(i + 1):
                    mm = nc.tensor.transpose(PS[2 + u % 2][:, j * P:(j + 1) * P], fs[u % 3][:, j * P:(j + 1) * P], identf[:, :])
                mm.then_inc(pt_ps, 1)

            def pv(u):
                h, i = divmod(u, ST)
                pe.wait_ge(pt_dve if u % 2 == 0 else pt_act, u // 2 + 1)
                if u >= 2:
                    pe.wait_ge(o_sb, u - 1)
                for j in range(i + 1):
                    mm = nc.tensor.matmul(PS[4 + u % 2][:, 0:FD], fpT[u % 2][:, j * P:(j + 1) * P],
                                          v[:, j, h * FD:(h + 1) * FD], start=j == 0, stop=j == i)
                mm.then_inc(o_ps, 1)

            pe.wait_ge(consts, 5)
            pe.wait_ge(proj_out, XKV0)
            pe.wait_ge(state_step, 1 + HP * NCH)
            pe.wait_ge(ho_sb, HP)
            pe.wait_ge(ho_rs, HP)
            pe.wait_ge(turn_sb, TURN0[2])

            def turn_fo(n, c, bank):
                pe.wait_ge(f_normed, 2 * c + 2)
                if n < 3:
                    pe.wait_ge(proj_out, XKV0 + sum(k <= list(FO_AT)[n] for k in KV_AT))
                    if n:
                        pe.wait_ge(cat_out, n)
                for t in range(ST):
                    mm = nc.tensor.transpose(bank[:, t * P:(t + 1) * P], fo[:, t, c * P:(c + 1) * P], identf[:, :])
                mm.then_inc(fo_turned, 1)

            negc(0)
            for u in range(FH * ST + LAG + 1):
                if u < FH * ST:
                    qk(u)
                if u % ST == 1 and u // ST + 1 < FH:
                    negc(u // ST + 1)
                if LAG <= u < FH * ST + LAG:
                    pt(u - LAG)
                if u > LAG:
                    pv(u - LAG - 1)
                if u in FO_AT:
                    turn_fo(list(FO_AT).index(u), FO_AT[u], PS[7])
                if u in KV_AT:
                    k = KV_AT.index(u)
                    if sum(a < u for a in FO_AT):
                        pe.wait_ge(cat_out, sum(a < u for a in FO_AT))
                    if k < DC:
                        g = run([across(2 + k // 4, P * (k % 4), src=memT, n=M)], g, 6 + k // 4)
                    else:
                        q = (k - DC) // MT
                        g = run([along(q, (k - DC) % MT, 0, 512, src=memT)], g, 8 + q)
            pe.wait_ge(proj_out, XQ0 - 1)
            def logits_of(t):
                pe.wait_ge(turn_sb, TURN0[3] + 2 * t + 2)
                pe.wait_ge(router_in, 16 * 4)
                for c in range(DC):
                    mm = nc.tensor.matmul(PS[4 + 2 * t % 4][0:NG + EX, 0:P], wgr[:, c, :], hT[:, c, t * P:(t + 1) * P],
                                          start=c == 0, stop=c == DC - 1)
                mm.then_inc(lgt_ps, 1)

            def project_some(base, n_load, src, k, chunks, first=True, last=True):
                t, n = divmod(k, 2)
                if k >= 4 and first:
                    pe.wait_ge(x1_done, base + k - 3)
                for j, c in enumerate(chunks):
                    mm = nc.tensor.matmul(PS[k % 4][:, :], src[:, c, t * P:(t + 1) * P], W[:, (n_load + n) % SLOTS, c, :],
                                          start=first and j == 0, stop=last and j == len(chunks) - 1)
                if last:
                    mm.then_inc(wout_ps, 1)

            def project_out(base, n_load, src, order, stage, begun=0):
                for q in range(2):
                    loaded(pe, n_load + q)
                for t in range(ST + 1):
                    if t < ST:
                        for n in range(2):
                            if 2 * t + n >= begun:
                                project_some(base, n_load, src, 2 * t + n, order)
                    if t == ST and stage == 2:
                        pe.wait_ge(x1_done, 5)
                        run([along(1, MT - 1, 0, 512, src=memT)], XQ0 - 1, 9)
                    if t >= 1:
                        turn_tile_pe(stage, t - 1, nA)
                    if t >= 2 and stage == 3:
                        for u in ([t - 2] if t < ST else [t - 2, t - 1]):
                            logits_of(u)

            pe.wait_ge(ho_step, 4)
            pe.wait_ge(co_done, 2)
            pe.wait_ge(s_done, FH * ST)
            pe.wait_ge(pt_dve, FH * ST // 2)
            pe.wait_ge(pt_act, FH * ST // 2)
            pe.wait_ge(cat_out, 3)
            loaded(pe, 10)
            loaded(pe, 11)
            order = [6, 7, 4, 5, 1, 0, 2]
            for k in range(2):
                project_some(0, 10, catT, k, order, last=False)
            pe.wait_ge(negc_sb, FH)
            turn_fo(3, 3, PS[6])
            project_some(0, 10, catT, 2, order, last=False)
            pe.wait_ge(cat_out, 4)
            for k in range(3):
                project_some(0, 10, catT, k, [3], first=False)
            pe.wait_ge(o_sb, FH * ST)
            project_out(0, 10, catT, order + [3], 2, begun=3)
            pe.wait_ge(turn_sb, TURN0[3])
            pe.wait_ge(x1_done, 8)
            g = run([across(0, P * c) for c in range(4)], g + 1, 12)
            g = run([across(1, P * c) for c in range(4)], g, 13)
            pe.wait_ge(proj_out, GROUPS_END)

            def x_scores(u):
                h, t = divmod(u, ST)
                if u >= 2:
                    pe.wait_ge(xe_done, u - 1)
                for k in range(2):
                    mm = nc.tensor.matmul(PS[u % 2][:, 0:M], xqT[:, 2 * h + k, t * P:(t + 1) * P], xkT[:, 2 * h + k, :],
                                          start=k == 0, stop=k == 1)
                mm.then_inc(xs_ps, 1)

            def x_turn(h):
                pe.wait_ge(xn_done, ST * (h + 1))
                for m in range(2):
                    if h:
                        pe.wait_ge(xpt_sb, 2 * (h - 1) + m + 1)
                    for t in range(ST):
                        mm = nc.tensor.transpose(PS[4 + m][:, t * P:(t + 1) * P], xp[:, h % 2, t, m * P:(m + 1) * P], identf[:, :])
                    mm.then_inc(xpt_ps, 1)

            def x_pv(h):
                pe.wait_ge(xpt_sb, 2 * h + 2)
                for n in range(2):
                    gg = 2 * h + n
                    if h:
                        pe.wait_ge(xo_sb, gg - 1)
                    for m in range(2):
                        mm = nc.tensor.matmul(PS[6 + n][:, :], xv[:, m, (2 * h + n) * P:(2 * h + n + 1) * P],
                                              xpT[:, (2 * h + m) % 4, :], start=m == 0, stop=m == 1)
                    mm.then_inc(xo_ps, 1)

            for h in range(XH + 1):
                for t in range(ST):
                    if h < XH:
                        x_scores(h * ST + t)
                    if t == 1 and h:
                        x_turn(h - 1)
                if h:
                    x_pv(h - 1)
            pe.wait_ge(xo_sb, 8)
            project_out(8, 14, xoT, list(range(DC)), 3)
            experts_pe(pe)


_INS = ["x", "mem", "mix_norm_g", "w_in", "fox_f_bias", "fox_norm_g", "hgrn_lb_logits", "hgrn_norm_g", "conv_w",
        "conv_b", "conv_norm_g", "conv_norm_b", "w_out", "xatt_norm_g", "mem_norm_g", "w_xq", "w_xkv", "w_xo",
        "ffn_norm_g", "w_group", "b_group", "w_router", "b_router", "w_gate", "w_up", "w_down", "final_norm_g"]


def kernel(**inputs):
    import numpy as _np
    import concourse.bacc as _bacc
    from concourse.bass_utils import run_bass_kernel_spmd as _run

    nc = _bacc.Bacc("TRN2", target_bir_lowering=False, num_devices=1)
    arrays, args = {}, []
    for name in _INS:
        a = _np.ascontiguousarray(inputs[name])
        arrays[f"in_{name}_dram"] = a
        args.append(nc.dram_tensor(f"in_{name}_dram", a.shape, mybir.dt.from_np(a.dtype), kind="ExternalInput").ap())
    args.append(nc.dram_tensor("out_0_dram", (1, S, D), F32, kind="ExternalOutput").ap())
    build(nc, *args)
    r = _run(nc, [arrays], core_ids=[0])
    return r.results[0]["out_0_dram"]
```
